# Optimizing a Trainium2 kernel written in Bass

```python
import jax, jax.numpy as jnp
from jax import lax
import numpy as np

D_MODEL = 1024
BATCH = 1
SEQ = 4096
DEPTH = 1

CHUNK = 64
PLE_DIM = 256
GLA_HEADS = 4
GLA_DK = 64
GLA_DV = 128
GLA_WIDTH = GLA_HEADS * GLA_DV
GLA_QK = GLA_HEADS * GLA_DK
GATE_RANK = 16
GATE_TAU = 16.0
CONV_WIDTH = 512
CONV_K = 3
D_MIX = GLA_WIDTH + CONV_WIDTH
SPLITS = [GLA_QK, GLA_QK, GLA_WIDTH, GLA_WIDTH, GATE_RANK,
          CONV_WIDTH, CONV_WIDTH, CONV_WIDTH, CONV_WIDTH]
D_IN = int(sum(SPLITS))
EPS = 1e-6

kernel_name = "hybrid_gla_shortconv_block"

def _rmsnorm(x, w):
    xf = x.astype(jnp.float32)
    y = xf * lax.rsqrt(jnp.mean(xf * xf, axis=-1, keepdims=True) + EPS)
    return (y * w.astype(jnp.float32)).astype(x.dtype)

def _gla_chunked(q, k, v, log_a):
    b, s, h, dk = q.shape
    dv = v.shape[-1]
    nc = s // CHUNK
    qc = q.reshape(b, nc, CHUNK, h, dk).astype(jnp.float32)
    kc = k.reshape(b, nc, CHUNK, h, dk).astype(jnp.float32)
    vc = v.reshape(b, nc, CHUNK, h, dv).astype(jnp.float32)
    cum = jnp.cumsum(log_a.reshape(b, nc, CHUNK, h, dk).astype(jnp.float32), axis=2)
    cum_end = cum[:, :, -1:]
    k_dec = kc * jnp.exp(cum_end - cum)
    gamma = jnp.exp(cum_end[:, :, 0])
    d_state = jnp.einsum('bnchk,bnchv->bnhkv', k_dec, vc)

    def step(state, inp):
        g, ds = inp
        state = g[..., None] * state + ds
        return state, state

    init = jnp.zeros((b, h, dk, dv), jnp.float32)
    _, states = lax.scan(step, init, (jnp.moveaxis(gamma, 1, 0), jnp.moveaxis(d_state, 1, 0)))
    states = jnp.moveaxis(states, 0, 1)
    o = jnp.einsum('bnchk,bnhkv->bnchv', qc, states)
    return o.reshape(b, s, h, dv).astype(q.dtype)

def _causal_depthwise_conv(u, w, bias):
    up = jnp.pad(u, ((0, 0), (CONV_K - 1, 0), (0, 0)))
    s = u.shape[1]
    out = bias
    for j in range(CONV_K):
        out = out + w[j] * up[:, j:j + s]
    return out

def setup_inputs(seed: int = 0) -> dict:
    key = jax.random.key(seed)
    ks = jax.random.split(key, 16)
    f32 = jnp.float32
    x = jax.random.normal(ks[0], (BATCH, SEQ, D_MODEL), f32)
    p = jax.random.normal(ks[1], (DEPTH, BATCH, SEQ, PLE_DIM), f32)
    norm_w = 1.0 + 0.02 * jax.random.normal(ks[2], (DEPTH, D_MODEL), f32)
    w_in = jax.random.normal(ks[3], (DEPTH, D_MODEL, D_IN), f32) * D_MODEL ** -0.5
    w_alpha_up = jax.random.normal(ks[4], (DEPTH, GATE_RANK, GLA_QK), f32) * GATE_RANK ** -0.5
    b_alpha = 0.5 + 0.1 * jax.random.normal(ks[5], (DEPTH, GLA_QK), f32)
    gla_norm_w = 1.0 + 0.02 * jax.random.normal(ks[6], (DEPTH, GLA_DV), f32)
    conv_w = jax.random.normal(ks[7], (DEPTH, CONV_K, CONV_WIDTH), f32) * CONV_K ** -0.5
    conv_b = 0.02 * jax.random.normal(ks[8], (DEPTH, CONV_WIDTH), f32)
    w_out = jax.random.normal(ks[9], (DEPTH, D_MIX, D_MODEL), f32) * D_MIX ** -0.5
    w_ple = jax.random.normal(ks[10], (DEPTH, PLE_DIM, D_MODEL), f32) * PLE_DIM ** -0.5
    w_ple_gate = jax.random.normal(ks[11], (DEPTH, D_MODEL, D_MODEL), f32) * D_MODEL ** -0.5
    b_ple_gate = 0.02 * jax.random.normal(ks[12], (DEPTH, D_MODEL), f32)
    final_norm_w = 1.0 + 0.02 * jax.random.normal(ks[13], (D_MODEL,), f32)
    return {"x": x, "p": p, "norm_w": norm_w, "w_in": w_in, "w_alpha_up": w_alpha_up,
            "b_alpha": b_alpha, "gla_norm_w": gla_norm_w, "conv_w": conv_w, "conv_b": conv_b,
            "w_out": w_out, "w_ple": w_ple, "w_ple_gate": w_ple_gate, "b_ple_gate": b_ple_gate,
            "final_norm_w": final_norm_w}

def reference(x, p, norm_w, w_in, w_alpha_up, b_alpha, gla_norm_w, conv_w, conv_b,
              w_out, w_ple, w_ple_gate, b_ple_gate, final_norm_w):
    b, s, _ = x.shape
    idx = list(np.cumsum(SPLITS)[:-1])
    h = x
    for i in range(DEPTH):
        n = _rmsnorm(h, norm_w[i])
        z = n @ w_in[i]
        q, k, v, g_gla, a_low, cb, cc, cu, g_conv = jnp.split(z, idx, axis=-1)

        log_a = jax.nn.log_sigmoid((a_low @ w_alpha_up[i] + b_alpha[i]).astype(jnp.float32)) / GATE_TAU
        qh = q.reshape(b, s, GLA_HEADS, GLA_DK) * (GLA_DK ** -0.5)
        kh = k.reshape(b, s, GLA_HEADS, GLA_DK)
        vh = v.reshape(b, s, GLA_HEADS, GLA_DV)
        o_gla = _gla_chunked(qh, kh, vh, log_a.reshape(b, s, GLA_HEADS, GLA_DK))
        o_gla = _rmsnorm(o_gla, gla_norm_w[i]).reshape(b, s, GLA_WIDTH)
        y_gla = o_gla * jax.nn.silu(g_gla)

        y_conv = cb * _causal_depthwise_conv(cc * cu, conv_w[i], conv_b[i])
        y_conv = y_conv * jax.nn.silu(g_conv)

        h = h + jnp.concatenate([y_gla, y_conv], axis=-1) @ w_out[i]

        gate = jax.nn.sigmoid(h @ w_ple_gate[i] + b_ple_gate[i])
        h = h + gate * (p[i] @ w_ple[i])
    return _rmsnorm(h, final_norm_w)


_drawn_inputs = setup_inputs


def setup_inputs(seed=0):
    import zlib

    import numpy as np

    out = dict(_drawn_inputs(seed))
    spreads = {}
    factors = {'norm_w': 2.899,
     'b_alpha': 3.218,
     'gla_norm_w': 178.832,
     'conv_b': 67.267,
     'b_ple_gate': 200.0,
     'final_norm_w': 20.592,
     'w_ple_gate': 30.256,
     'p': 7.363,
     'w_ple': 7.373}
    for name, (base, spread) in spreads.items():
        noise = np.random.default_rng([zlib.crc32(name.encode()), seed]).standard_normal(out[name].shape)
        drawn = base * np.exp(spread * noise) if base else spread * noise
        out[name] = __import__('jax').numpy.asarray(drawn.astype(out[name].dtype))
    for name, factor in factors.items():
        out[name] = (out[name] * factor).astype(out[name].dtype)
    return out
```

```python
from contextlib import ExitStack

import concourse.bass as bass
from concourse import mybir

P = 128
D_MODEL, SEQ = 1024, 4096
TB = 512
NB = SEQ // TB
KT = D_MODEL // P
HEADS, DK, DV = 4, 64, 128
QK, RANK, CHUNK = HEADS * DK, 16, 64
KA = QK + RANK
TT = TB // P
NCH = TB // CHUNK
PLE_K = 2
EPS = 1e-6
SLOTS = 16
BIG = D_MODEL * 4

F32 = mybir.dt.float32
F32R = mybir.dt.float32r
ACT = mybir.ActivationFunctionType
ALU = mybir.AluOpType

GLA, CONV, OUT, GATE = range(4)

V_NORM, V_GLA, V_CW, V_CB, V_BG, V_FIN = 0, 8, 9, 21, 25, 33
N_VEC = 41

W_KA, W_V, W_Q, W_G, W_CONV, W_OUT, W_GATE, W_PLE, N_W = 0, 4, 8, 10, 14, 30, 38, 46, 48
KA_SLOT = 10
RING_ORDER = [10, 11, 12, 0, 1, 2, 3, 4, 5, 6, 7, 8, 9, 13, 14, 15]


def slot_of(n):
    if n < W_CONV:
        return n - W_V
    if n < W_OUT:
        return RING_ORDER[n - W_CONV]
    if n < W_PLE:
        return RING_ORDER[n - W_OUT]
    return RING_ORDER[n - W_PLE]


MAIN = (0, 1, 2)
O_BANK = (3, 4)
DS_BANK = (5, 6)
SMALL = 7
TURN = (0, 1, 2, 5, 6, 7, 3, 4)
STAT = 6

H_RECIP, H_SCALED, H_DONE = 1, 2, 3
C_CARRY, C_U, C_W0, C_W1, C_W2, C_GATED, C_DONE = range(1, 8)
TILES = {GLA: 14, CONV: 16, OUT: 8, GATE: 16}


def build(nc, xb, pb, w_ka, w_in, w_out, w_gate, w_ple, w_up, b_alpha, vectors, masks,
          out, y_scratch, h_scratch, r_scratch):
    with ExitStack() as ctx:
        def sb(name, shape, dt=F32):
            return ctx.enter_context(nc.sbuf_tensor(name, shape, dt))

        def sem(name):
            return ctx.enter_context(nc.semaphore(name))

        def over(name, shape, at, dt=F32):
            return nc.alloc_sbuf_tensor_at(name, shape, dt, offset=at)

        ps = [ctx.enter_context(nc.psum_tensor(f"bank{i}", [P, 512], F32)) for i in range(8)]

        wh_at = (nc.sbuf_base + 31) // 32 * 32
        WH = sb("WH", [P, SLOTS, KT, P], F32R)
        wl_at = wh_at + SLOTS * BIG
        WL = sb("WL", [P, SLOTS, KT, P], F32R)
        XH = sb("XH", [P, KT, TB], F32R)
        XL = sb("XL", [P, KT, TB], F32R)
        raw = sb("raw", [P, KT, TB])
        stage = sb("stage", [P, 2, D_MODEL])
        vec = sb("vec", [P, N_VEC])
        eps = sb("eps", [P, 1])
        mask = sb("mask", [P, 2 * P + 2])
        ones = sb("ones", [P, P])
        bias2 = sb("bias2", [P, 2 * QK])
        wup = sb("wup", [RANK, QK])
        y_sb = sb("y_sb", [P, 2, TB])
        R = sb("R", [P, TB])
        suffix, ident, member = mask[:, 0:P], mask[:, P:2 * P], mask[:, 2 * P:2 * P + 2]

        KAH = WH[:, KA_SLOT:KA_SLOT + 3].rearrange("p s k c -> p (s k c)")[:, 0:KT * KA].rearrange(
            "p (k c) -> p k c", k=KT)
        KAL = WL[:, KA_SLOT:KA_SLOT + 3].rearrange("p s k c -> p (s k c)")[:, 0:KT * KA].rearrange(
            "p (k c) -> p k c", k=KT)
        v_sb = over("v_sb", [P, TT, HEADS * DV], wh_at + 13 * BIG)
        hist = over("hist", [P, NCH, 2, DV], wl_at + 13 * BIG)
        L = over("L", [P, TT, QK], wh_at + 15 * BIG)
        q_sb = over("q_sb", [P, 2, TB], wl_at + 15 * BIG)
        raw_odd = over("raw_odd", [P, KT, TB], wh_at)
        raws = (raw, raw_odd)

        ROW = TB * 4
        a_at = (nc.sbuf_base + 31) // 32 * 32
        region_a = sb("region_a", [P, 14592 // 4])
        ka_sb = over("ka_sb", [P, TT, KA], a_at)
        aT = over("aT", [RANK, TB], a_at + 4352)
        tmp = over("tmp", [P, 2, TB], a_at + 4352 + ROW)
        sq = over("sq", [P, 2, TB], a_at + 4352 + 3 * ROW)
        u = over("u", [P, 4, 2 + TB], a_at)
        ccs = over("ccs", [P, TB], a_at + 8224)
        cv = over("cv", [P, TB], a_at + 8224 + ROW)
        sgc = over("sgc", [P, TB], a_at + 8224 + 2 * ROW)
        p_raw = over("p_raw", [P, PLE_K, TB], a_at)
        PH = over("PH", [P, PLE_K, TB], a_at + 2 * ROW, F32R)
        PL = over("PL", [P, PLE_K, TB], a_at + 4 * ROW, F32R)
        t_sb = over("t_sb", [P, TB], a_at + 6 * ROW)
        b_at = (nc.sbuf_base + 31) // 32 * 32
        region_b = sb("region_b", [P, 12288 // 4])
        sg = over("sg", [P, HEADS, TB], b_at)
        hsq = over("hsq", [P, TB], b_at + 4 * ROW)
        rt = over("rt", [P, TB], b_at + 5 * ROW)
        xt = over("xt", [P, 4, TB], b_at)
        acc = over("acc", [P, TB], b_at)
        gt = over("gt", [P, 2, TB], b_at + 4 * ROW)
        osq = y_sb
        gamma = sb("gamma", [P, 2, NCH])
        sqs = (tmp[:, 0], tmp[:, 1], sq[:, 0], sq[:, 1])

        consts_loaded = sem("consts_loaded")
        memsets = sem("memsets")
        stage_loaded = [sem(f"stage_loaded{i}") for i in range(2)]
        w_hi = sem("w_hi")
        w_ready = sem("w_ready")
        raw_loaded = [sem(f"raw_loaded{i}") for i in range(4)]
        n_ready = sem("n_ready")
        x_hi = sem("x_hi")
        x_lo = sem("x_lo")
        x_free = sem("x_free")
        tile_done = [sem(f"tile_done_{n}") for n in ("gla", "conv", "out", "gate")]
        x_sq = sem("x_sq")
        x_sum = sem("x_sum")
        x_mean = sem("x_mean")
        x_root = sem("x_root")
        x_rstd = sem("x_rstd")
        r_stored = sem("r_stored")
        r_loaded = sem("r_loaded")
        evacuated = sem("evacuated")
        aT_done = sem("aT_done")
        aT_ready = sem("aT_ready")
        z_done = sem("z_done")
        z_ready = sem("z_ready")
        z_neg = sem("z_neg")
        z_exp = sem("z_exp")
        z_log = sem("z_log")
        loga = sem("loga")
        cum_done = sem("cum_done")
        decay = sem("decay")
        kdec = sem("kdec")
        gm_done = sem("gm_done")
        gamma_ready = sem("gamma_ready")
        ds_done = sem("ds_done")
        s_updated = sem("s_updated")
        o_done = sem("o_done")
        head_sq = sem("head_sq")
        head_mean = sem("head_mean")
        head_root = sem("head_root")
        head_step = sem("head_step")
        y_stored = [sem(f"y_stored{i}") for i in range(2)]
        cc_copied = sem("cc_copied")
        silu_ready = sem("silu_ready")
        conv_step = sem("conv_step")
        xt_loaded = [sem(f"xt_loaded{i}") for i in range(4)]
        h_ready = sem("h_ready")
        h_stored = [sem(f"h_stored{i}") for i in range(4)]
        p_loaded = sem("p_loaded")
        p_hi = sem("p_hi")
        p_lo = sem("p_lo")
        gate_ready = sem("gate_ready")
        gated = sem("gated")
        mixed = sem("mixed")
        out_sq = sem("out_sq")
        out_sum = sem("out_sum")
        out_mean = sem("out_mean")
        out_root = sem("out_root")
        out_rstd = sem("out_rstd")
        out_norm = sem("out_norm")
        out_stored = [sem(f"out_stored{i}") for i in range(4)]

        def wait_tile(eng, phase, b, i):
            if i == TILES[phase] - 1:
                eng.wait_ge(x_free, 8 * (8 * phase + b + 1))
            else:
                eng.wait_ge(tile_done[phase], (TILES[phase] - 1) * b + i + 1)

        def over_blocks(eng, body, pair=False, apart=1):
            for b in range(apart):
                body(b)
            if pair:
                with eng.Fori(1, NB - 2, 2) as b:
                    body(b, 1)
                    body(b + 1, 0)
            else:
                with eng.Fori(apart, NB - 1) as b:
                    body(b)
            body(NB - 1, 1) if pair else body(NB - 1)

        def is_first(b):
            return isinstance(b, int) and b == 0

        def is_last(b):
            return isinstance(b, int) and b == NB - 1

        block = ctx.enter_context(nc.Block())

        @block.sync
        def _(sp):
            def load_raw(dst, src, step):
                for c in range(4):
                    sp.dma_start(dst[:, 2 * c:2 * c + 2], src[:, 2 * c:2 * c + 2]).then_inc(raw_loaded[c], 16)

            def store_y(n, b, k):
                sp.dma_start(y_scratch[b, :, k], y_sb[:, k % 2]).then_inc(y_stored[k % 2], 16)

            def store_r(b):
                sp.wait_ge(x_rstd, b + 1)
                sp.dma_start(r_scratch[b], R[:]).then_inc(r_stored, 16)

            def store_heads(b):
                for h in range(HEADS):
                    sp.wait_ge(head_step, 3 * (4 * b + h) + H_DONE)
                    store_y(4 * b + h, b, h)

            def gla(b):
                sp.wait_ge(x_lo, 8 * (b + 1))
                load_raw(raw, xb[0] if is_last(b) else xb[b + 1], b + 1)
                if not is_first(b):
                    store_heads(b - 1)
                if is_last(b):
                    sp.wait_ge(r_stored, 16 * NB)
                    sp.wait_ge(n_ready, 8 * NB)
                    sp.dma_start(R[:], r_scratch[0]).then_inc(r_loaded, 16)
                else:
                    store_r(b + 1)

            def conv(b):
                sp.wait_ge(x_lo, 8 * (NB + b + 1))
                if is_last(b):
                    sp.wait_ge(y_stored[0], 16 * (2 * NB + 2 * (NB - 1)))
                    sp.wait_ge(y_stored[1], 16 * (2 * NB + 2 * (NB - 1)))
                    load_raw(raw, y_scratch[0], 2 * NB)
                else:
                    load_raw(raw, xb[b + 1], NB + b + 1)
                    sp.wait_ge(n_ready, 8 * (NB + b + 1))
                    sp.dma_start(R[:], r_scratch[b + 1]).then_inc(r_loaded, 16)
                if is_first(b):
                    store_heads(NB - 1)
                for j in range(4):
                    sp.wait_ge(conv_step, 7 * (4 * b + j) + C_DONE)
                    store_y(4 * NB + 4 * b + j, b, 4 + j)

            def load_xt(b, m):
                sp.dma_start(xt[:, m % 4], xb[b, :, m]).then_inc(xt_loaded[m % 4], 16)

            def out_proj(b):
                sp.wait_ge(x_lo, 8 * (2 * NB + b + 1))
                if is_last(b):
                    for c in range(4):
                        sp.wait_ge(h_stored[c], 16 * 2 * (NB - 1))
                    load_raw(raw, h_scratch[0], 3 * NB)
                    sp.dma_start(p_raw[:], pb[0]).then_inc(p_loaded, 16)
                else:
                    for c in range(2):
                        sp.wait_ge(y_stored[c], 16 * 4 * NB)
                    load_raw(raw, y_scratch[b + 1], 2 * NB + b + 1)
                for m in range(KT):
                    sp.wait_ge(h_ready, 8 * b + m + 1)
                    sp.dma_start(h_scratch[b, :, m], xt[:, m % 4]).then_inc(h_stored[m % 4], 16)
                    if is_last(b) and m + 2 >= KT:
                        continue
                    if not is_first(b) or m >= 2:
                        sp.wait_ge(h_stored[(m + 2) % 4], 16 * (2 * b + (m + 2) // 4))
                    if m + 2 < KT:
                        load_xt(b, m + 2)
                    else:
                        load_xt(b + 1, m + 2 - KT)

            def store_out(b, odd):
                for c in range(4):
                    sp.wait_ge(out_norm, 8 * b + 2 * c + 2)
                    sp.dma_start(out[b, :, 2 * c:2 * c + 2], raws[odd][:, 2 * c:2 * c + 2]).then_inc(
                        out_stored[c], 16)

            def gate(b, odd=0):
                if not is_last(b):
                    sp.wait_ge(p_lo, 2 * (b + 1))
                    sp.dma_start(p_raw[:], pb[b + 1]).then_inc(p_loaded, 16)
                if is_first(b):
                    sp.wait_ge(x_free, 8 * 3 * NB)
                    for c in range(4):
                        sp.wait_ge(h_stored[c], 16 * 2 * NB)
                else:
                    store_out(b - 1, 1 - odd)
                if not is_last(b):
                    if not is_first(b):
                        for c in range(4):
                            sp.wait_ge(out_stored[c], 16 * b)
                    load_raw(raws[1 - odd], h_scratch[b + 1], 3 * NB + b + 1)

            load_raw(raw, xb[0], 0)
            sp.dma_start(vec[:], vectors).then_inc(consts_loaded, 16)
            sp.dma_start(mask[:], masks).then_inc(consts_loaded, 16)
            sp.dma_start(bias2[:], b_alpha).then_inc(consts_loaded, 16)
            sp.dma_start(wup[:], w_up).then_inc(consts_loaded, 16)
            store_r(0)
            over_blocks(sp, gla, apart=2)
            over_blocks(sp, conv)
            load_xt(0, 0)
            load_xt(0, 1)
            over_blocks(sp, out_proj)
            over_blocks(sp, gate, pair=True)
            store_out(NB - 1, 1)
            for c in range(4):
                sp.wait_ge(out_stored[c], 16 * NB)

        @block.gpsimd
        def _(pool):
            pool.memset(ones[:], 1.0).then_inc(memsets, 1)
            pool.memset(eps[:], EPS).then_inc(memsets, 1)
            pool.memset(hist[:, NCH - 1], 0.0).then_inc(memsets, 1)

            def source(n):
                if n < W_V:
                    return w_ka[:, 2 * n:2 * n + 2].rearrange("p k c -> p (k c)")
                if n < W_OUT:
                    return w_in[n - W_V]
                if n < W_GATE:
                    return w_out[n - W_OUT]
                if n < W_PLE:
                    return w_gate[n - W_GATE]
                return w_ple[n - W_PLE]

            def load(n):
                if n >= 2:
                    pool.wait_ge(w_ready, n - 1)
                src = source(n)
                pool.dma_start(stage[:, n % 2, 0:src.shape[1]], src).then_inc(stage_loaded[n % 2], 16)

            def wait_slot_free(n):
                if n < W_CONV:
                    return
                if n < W_OUT:
                    s = slot_of(n)
                    if s >= 13:
                        pool.wait_ge(o_done, HEADS * NB)
                    elif s >= KA_SLOT:
                        wait_tile(pool, GLA, NB - 1, 3)
                    elif s < 4:
                        wait_tile(pool, GLA, NB - 1, 7)
                    else:
                        wait_tile(pool, GLA, NB - 1, 4 + s)
                elif n < W_PLE:
                    wait_tile(pool, CONV, NB - 1, n - W_OUT)
                else:
                    wait_tile(pool, OUT, NB - 1, n - W_PLE)

            load(0)
            for n in range(N_W):
                if n + 1 < N_W:
                    load(n + 1)
                pool.wait_ge(stage_loaded[n % 2], 16 * (n // 2 + 1))
                wait_slot_free(n)
                if n < W_V:
                    hi, lo = KAH[:, 2 * n:2 * n + 2], KAL[:, 2 * n:2 * n + 2]
                    src = stage[:, n % 2, 0:2 * KA].rearrange("p (k c) -> p k c", k=2)
                else:
                    hi, lo = WH[:, slot_of(n)], WL[:, slot_of(n)]
                    src = stage[:, n % 2].rearrange("p (k c) -> p k c", k=KT)
                pool.tensor_scalar(hi, src, 1.0, 0.0, ALU.mult, ALU.add).then_inc(w_hi, 1)
                pool.wait_ge(w_hi, n + 1)
                pool.tensor_tensor(lo, src, hi.bitcast(F32), ALU.subtract).then_inc(w_ready, 1)

        @block.tensor
        def _(pe):
            def big_tile(phase, b, i, acc_ap, products, half=None, waits=None):
                step = 8 * phase + b
                last = i == TILES[phase] - 1
                first = i == (1 if phase == GATE else 0)
                for k in range(KT):
                    hh, lh, hl = products(k)
                    if first:
                        pe.wait_ge(x_hi, 8 * step + k + 1)
                    nc.tensor.matmul(acc_ap, hh[0], hh[1], start=(k == 0), stop=False)
                    if lh[2]:
                        nc.tensor.matmul(acc_ap, lh[0], lh[1], start=False, stop=False)
                    if first:
                        pe.wait_ge(x_lo, 8 * step + k + 1)
                    if not lh[2]:
                        nc.tensor.matmul(acc_ap, lh[0], lh[1], start=False, stop=False)
                    if waits is not None:
                        waits(k)
                    mm = nc.tensor.matmul(acc_ap, hl[0], hl[1], start=False, stop=(k == KT - 1))
                    if last:
                        mm.then_inc(x_free, 1)
                    elif k == KT - 1:
                        mm.then_inc(tile_done[phase], 1)
                    if k == 3 and half is not None:
                        half()

            def stationary_w(slot):
                return lambda k: ((WH[:, slot, k], XH[:, k], True), (WL[:, slot, k], XH[:, k], True),
                                  (WH[:, slot, k], XL[:, k], True))

            def weights(b, n):
                if is_first(b):
                    pe.wait_ge(w_ready, n + 1)

            def mean_of(bank, src):
                return nc.tensor.matmul(ps[bank][:], ones[:], src, start=True, stop=True)

            def x_stats(s):
                pe.wait_ge(x_sum, 8 * (s + 1))
                mean_of(SMALL, R[:]).then_inc(x_mean, 1)

            def main_bank(b, i):
                if i >= 3:
                    pe.wait_ge(evacuated, 14 * b + i - 2)
                elif not is_first(b):
                    pe.wait_ge(evacuated, 14 * b - (1, 0, 2)[i] if i != 2 else 14 * b - 2)
                return ps[MAIN[i % 3]]

            def ka_tile(b, t):
                if is_first(b):
                    pe.wait_ge(w_ready, W_V)
                tok = slice(t * P, t * P + P)
                big_tile(GLA, b, t, main_bank(b, t)[:, 0:KA],
                         lambda k: ((XH[:, k, tok], KAH[:, k], True), (XH[:, k, tok], KAL[:, k], True),
                                    (XL[:, k, tok], KAH[:, k], True)))

            def v_tile(b, t, half=None):
                if is_first(b):
                    pe.wait_ge(w_ready, W_Q)
                tok = slice(t * P, t * P + P)
                bank = main_bank(b, 4 + t)[:, :].rearrange("p (s c) -> p s c", s=4)
                big_tile(GLA, b, 4 + t, bank,
                         lambda k: ((XH[:, k, tok], WH[:, 0:4, k], True), (XH[:, k, tok], WL[:, 0:4, k], True),
                                    (XL[:, k, tok], WH[:, 0:4, k], True)), half)

            def gla_tile(b, i, n, half=None, waits=None):
                weights(b, n)
                big_tile(GLA, b, i, main_bank(b, i)[:], stationary_w(slot_of(n)), half, waits)

            def head_out(b, h):
                rows = slice(DK * (h % 2), DK * (h % 2) + DK)
                if h == 0:
                    pe.wait_ge(s_updated, 2 * NCH * (b + 1))
                if h >= 2:
                    pe.wait_ge(head_step, 3 * (4 * b + h - 2) + H_SCALED)
                for c in range(NCH):
                    cols = slice(c * CHUNK, c * CHUNK + CHUNK)
                    mm = nc.tensor.matmul(ps[O_BANK[h % 2]][:, cols], hist[rows, c, h // 2],
                                          q_sb[rows, h // 2, cols], start=True, stop=True)
                mm.then_inc(o_done, 1)

            def head_stat(b, h):
                if h == 0:
                    pe.wait_ge(gamma_ready, b + 1)
                elif h == 2:
                    pass
                else:
                    pe.wait_ge(head_root, 4 * b + h)
                pe.wait_ge(head_sq, 4 * b + h + 1)
                mean_of(SMALL, hsq[:]).then_inc(head_mean, 1)

            def turn_a(b):
                pe.wait_ge(evacuated, 14 * b + 4)
                if is_first(b):
                    pe.wait_ge(x_root, 1)
                else:
                    pe.wait_ge(head_root, 4 * (b - 1) + 2)
                for t in range(TT):
                    mm = nc.tensor.transpose(ps[SMALL][0:RANK, t * P:t * P + P], ka_sb[:, t, QK:KA], ident)
                mm.then_inc(aT_done, 1)

            def logits(b, i):
                for t in range(2 * i, 2 * i + 2):
                    mm = nc.tensor.matmul(ps[SMALL][:, (t % 2) * QK:(t % 2) * QK + QK],
                                          aT[:, t * P:t * P + P], wup[:], start=True, stop=True)
                mm.then_inc(z_done, 1)

            def suffix_sums(b, i):
                for t in range(2 * i, 2 * i + 2):
                    mm = nc.tensor.matmul(ps[SMALL][:, (t % 2) * QK:(t % 2) * QK + QK],
                                          suffix, L[:, t], start=True, stop=True)
                mm.then_inc(cum_done, 1)

            def chunk_sums(b):
                for f in range(2):
                    for t in range(TT):
                        mm = nc.tensor.matmul(ps[SMALL][:, f * NCH + 2 * t:f * NCH + 2 * t + 2],
                                              L[:, t, f * P:f * P + P], member, start=True, stop=True)
                mm.then_inc(gm_done, 1)

            def increments(b, c):
                for ch in (c, c + 1):
                    rows = slice(CHUNK * (ch % 2), CHUNK * (ch % 2) + CHUNK)
                    for h in range(HEADS):
                        mm = nc.tensor.matmul(
                            ps[DS_BANK[ch % 2]][DK * (h % 2):DK * (h % 2) + DK, (h // 2) * DV:(h // 2) * DV + DV],
                            ka_sb[rows, ch // 2, h * DK:h * DK + DK],
                            v_sb[rows, ch // 2, h * DV:h * DV + DV], start=True, stop=True)
                    mm.then_inc(ds_done, 1)

            def increment_waits(b, c):
                if c == 0:
                    pe.wait_ge(kdec, 2 * b + 2)
                    pe.wait_ge(evacuated, 14 * b + 8)
                if not (is_first(b) and c == 0):
                    pe.wait_ge(s_updated, 2 * (NCH * b + c))

            def gla(b):
                tail = not is_first(b)
                if tail:
                    head_out(b - 1, 0)
                    head_out(b - 1, 1)
                ka_tile(b, 0)
                ka_tile(b, 1)
                if tail:
                    head_stat(b - 1, 0)
                ka_tile(b, 2)
                if tail:
                    head_stat(b - 1, 1)
                ka_tile(b, 3)
                if tail:
                    head_out(b - 1, 2)
                turn_a(b)

                def o3():
                    if tail:
                        head_out(b - 1, 3)

                def stat3():
                    if tail:
                        head_stat(b - 1, 3)
                v_tile(b, 0, o3)
                if tail:
                    pe.wait_ge(aT_ready, b + 1)
                    head_stat(b - 1, 2)
                v_tile(b, 1, stat3)
                pe.wait_ge(aT_ready, b + 1)
                if tail:
                    pe.wait_ge(head_root, 4 * b)
                logits(b, 0)
                v_tile(b, 2)
                pe.wait_ge(z_ready, 2 * b + 1)
                if not is_last(b):
                    x_stats(b + 1)

                def z1():
                    if not is_last(b):
                        pe.wait_ge(x_root, b + 2)
                    logits(b, 1)
                v_tile(b, 3, z1)
                gla_tile(b, 8, W_Q)
                pe.wait_ge(z_ready, 2 * b + 2)
                pe.wait_ge(loga, b + 1)
                suffix_sums(b, 0)

                def c1():
                    pe.wait_ge(decay, 2 * b + 1)
                    suffix_sums(b, 1)
                gla_tile(b, 9, W_Q + 1, c1)
                pe.wait_ge(decay, 2 * b + 2)
                chunk_sums(b)
                gla_tile(b, 10, W_G, waits=lambda k: increment_waits(b, 0) if k == 7 else None)
                increments(b, 0)
                gla_tile(b, 11, W_G + 1, lambda: increments(b, 2),
                         lambda k: increment_waits(b, {3: 2, 7: 4}[k]) if k in (3, 7) else None)
                increments(b, 4)
                gla_tile(b, 12, W_G + 2, lambda: increments(b, 6),
                         lambda k: increment_waits(b, 6) if k == 3 else None)
                gla_tile(b, 13, W_G + 3)

            def conv(b):
                for t in range(16):
                    n = W_CONV + t
                    weights(b, n)
                    if is_first(b) and t < 8:
                        if t < 3:
                            pe.wait_ge(evacuated, 14 * NB - (1, 0, 2)[t])
                        elif t < 5:
                            pe.wait_ge(s_updated, 2 * NCH * NB)
                        elif t == 5:
                            pe.wait_ge(head_root, HEADS * NB)
                        else:
                            pe.wait_ge(head_step, 3 * (HEADS * NB - 8 + t) + H_SCALED)
                    else:
                        wait_conv_read(4 * b - 2 + t // 4, t % 4)
                    big_tile(CONV, b, t, ps[TURN[t % 8]][:], stationary_w(slot_of(n)))
                    if is_first(b):
                        if t == 0:
                            head_out(NB - 1, 0)
                            head_out(NB - 1, 1)
                        if t == 1:
                            head_stat(NB - 1, 0)
                            head_stat(NB - 1, 1)
                        if t == 3:
                            head_out(NB - 1, 2)
                            head_out(NB - 1, 3)
                        if t == 4:
                            pe.wait_ge(head_root, HEADS * NB - 2)
                            head_stat(NB - 1, 2)
                            head_stat(NB - 1, 3)

            def wait_conv_read(j, kind):
                if kind == 0:
                    pe.wait_ge(cc_copied, j + 1)
                elif kind == 1:
                    pe.wait_ge(conv_step, 7 * j + C_U)
                elif kind == 2:
                    pe.wait_ge(silu_ready, j + 1)
                else:
                    pe.wait_ge(conv_step, 7 * j + C_GATED)

            def out_proj(b):
                for m in range(KT):
                    weights(b, W_OUT + m)
                    if is_first(b):
                        wait_conv_read(4 * NB - 2 + m // 4, m % 4)
                    else:
                        pe.wait_ge(h_ready, 8 * (b - 1) + m + 1)
                    big_tile(OUT, b, m, ps[TURN[m]][:], stationary_w(slot_of(W_OUT + m)))

            def wait_out_read(bank):
                pe.wait_ge(h_ready, 8 * (NB - 1) + TURN.index(bank) + 1)

            def gate(b, odd=0):
                for m in range(KT):
                    if is_first(b) and m == 0:
                        pe.wait_ge(w_ready, N_W)
                    if m == 0:
                        pe.wait_ge(p_hi, 2 * (b + 1))
                        pe.wait_ge(p_lo, 2 * (b + 1))
                    if is_first(b) and m < 3:
                        wait_out_read(3 + m)
                    else:
                        pe.wait_ge(gated, 8 * b + m - 2 if m >= 3 else 8 * b - (1, 0, 2)[m])
                    bank = ps[3 + m % 3][:]
                    for k in range(PLE_K):
                        s = slot_of(W_PLE + k)
                        nc.tensor.matmul(bank, WH[:, s, m], PH[:, k], start=(k == 0), stop=False)
                        nc.tensor.matmul(bank, WL[:, s, m], PH[:, k], start=False, stop=False)
                        mm = nc.tensor.matmul(bank, WH[:, s, m], PL[:, k], start=False, stop=(k == PLE_K - 1))
                    mm.then_inc(tile_done[GATE], 1)
                    weights(b, W_GATE + m)
                    if is_first(b) and m < 3:
                        wait_out_read(m)
                    else:
                        pe.wait_ge(gate_ready, 8 * b + m - 2 if m >= 3 else 8 * b - (1, 0, 2)[m])
                    big_tile(GATE, b, 2 * m + 1, ps[m % 3][:], stationary_w(slot_of(W_GATE + m)))
                    if m == 0 and not is_first(b):
                        out_stats(b - 1)

            def out_stats(b):
                pe.wait_ge(out_sum, 8 * (b + 1))
                mean_of(STAT, acc[:]).then_inc(out_mean, 1)

            pe.wait_ge(memsets, 3)
            pe.wait_ge(consts_loaded, 64)
            x_stats(0)
            over_blocks(pe, gla, apart=2)
            over_blocks(pe, conv)
            over_blocks(pe, out_proj)
            over_blocks(pe, gate, pair=True)
            out_stats(NB - 1)

        @block.scalar
        def _(act):
            def split_hi(step, src, phase):
                for k in range(KT):
                    if phase in (GLA, CONV):
                        act.wait_ge(n_ready, 8 * step + k + 1)
                    elif k % 2 == 0:
                        act.wait_ge(raw_loaded[k // 2], 16 * (step + 1))
                    if not (isinstance(step, int) and step == 0):
                        act.wait_ge(x_free, 8 * (step - 1) + k + 1)
                    nc.scalar.activation(XH[:, k], src[:, k], ACT.Copy).then_inc(x_hi, 1)

            def x_squares(s, ks):
                for k in ks:
                    if k % 2 == 0:
                        act.wait_ge(raw_loaded[k // 2], 16 * (s + 1))
                    if k < 4:
                        if not is_first(s):
                            act.wait_ge(x_sum, 8 * s)
                            if k < 2 and not (isinstance(s, int) and s == 1):
                                act.wait_ge(kdec, 2 * (s - 1))
                    else:
                        act.wait_ge(x_sum, 8 * s + k - 3)
                    nc.scalar.activation(sqs[k % 4], raw[:, k], ACT.Square).then_inc(x_sq, 1)

            def x_rms(s):
                act.wait_ge(x_mean, s + 1)
                nc.scalar.activation(R[:], ps[SMALL][:], ACT.Sqrt, bias=eps[:], scale=1.0 / D_MODEL).then_inc(
                    x_root, 1)

            def evacuate(b, i, dst, src, func=ACT.Copy, scale=1.0):
                wait_tile(act, GLA, b, i)
                nc.scalar.activation(dst, src, func, scale=scale).then_inc(evacuated, 1)

            def ka_out(b, t):
                if not is_first(b):
                    act.wait_ge(ds_done, NCH * b)
                evacuate(b, t, ka_sb[:, t], ps[MAIN[t % 3]][:, 0:KA])

            def v_out(b, t):
                if not is_first(b):
                    act.wait_ge(ds_done, NCH * b)
                evacuate(b, 4 + t, v_sb[:, t], ps[MAIN[(4 + t) % 3]][:])

            def q_out(b, t):
                if not is_first(b):
                    act.wait_ge(o_done, HEADS * b)
                evacuate(b, 8 + t, q_sb[:, t], ps[MAIN[(8 + t) % 3]][:], scale=DK ** -0.5)

            def g_out(b, h):
                if not is_first(b):
                    act.wait_ge(head_step, 3 * (4 * (b - 1) + h) + H_DONE)
                evacuate(b, 10 + h, sg[:, h], ps[MAIN[(10 + h) % 3]][:], ACT.Silu)

            def head_squares(b, h):
                act.wait_ge(o_done, 4 * b + h + 1)
                if h > 0:
                    act.wait_ge(head_mean, 4 * b + h)
                nc.scalar.activation(hsq[:], ps[O_BANK[h % 2]][:], ACT.Square).then_inc(head_sq, 1)

            def head_rms(b, h):
                act.wait_ge(head_mean, 4 * b + h + 1)
                if h > 0:
                    act.wait_ge(head_step, 3 * (4 * b + h - 1) + H_SCALED)
                nc.scalar.activation(rt[:], ps[SMALL][:], ACT.Sqrt, bias=eps[:], scale=1.0 / DV).then_inc(
                    head_root, 1)

            def a_out(b):
                act.wait_ge(aT_done, b + 1)
                if not is_first(b):
                    act.wait_ge(z_done, 2 * b)
                nc.scalar.activation(aT[:], ps[SMALL][0:RANK, :], ACT.Copy).then_inc(aT_ready, 1)

            def log_sigmoid(b):
                act.wait_ge(z_neg, b + 1)
                nc.scalar.activation(tmp[:], tmp[:], ACT.Exp).then_inc(z_exp, 1)

            def log_sigmoid_ln(b):
                act.wait_ge(z_exp, b + 1)
                nc.scalar.activation(tmp[:], tmp[:], ACT.Ln, bias=1.0).then_inc(z_log, 1)

            def decay_out(b, i):
                act.wait_ge(loga, b + 1)
                act.wait_ge(cum_done, 2 * b + i + 1)
                nc.scalar.activation(tmp[:, i], ps[SMALL][:], ACT.Exp).then_inc(decay, 1)

            def gamma_out(b):
                act.wait_ge(gm_done, b + 1)
                if not is_first(b):
                    act.wait_ge(s_updated, 2 * NCH * b)
                nc.scalar.activation(gamma[:].rearrange("p f c -> p (f c)"), ps[SMALL][:, 0:2 * NCH],
                                     ACT.Exp).then_inc(gamma_ready, 1)

            def gla(b):
                tail = not is_first(b)
                nxt = not is_last(b)
                if tail:
                    head_squares(b - 1, 0)
                ka_out(b, 0)
                ka_out(b, 1)
                if tail:
                    head_squares(b - 1, 1)
                    head_rms(b - 1, 0)
                ka_out(b, 2)
                ka_out(b, 3)
                if tail:
                    head_rms(b - 1, 1)
                a_out(b)
                if tail:
                    head_squares(b - 1, 2)
                v_out(b, 0)
                if tail:
                    head_squares(b - 1, 3)
                    head_rms(b - 1, 2)
                if nxt:
                    x_squares(b + 1, range(0, 4))
                if tail:
                    head_rms(b - 1, 3)
                v_out(b, 1)
                if nxt:
                    x_squares(b + 1, range(4, 8))
                v_out(b, 2)
                if nxt:
                    x_rms(b + 1)
                v_out(b, 3)
                log_sigmoid(b)
                log_sigmoid_ln(b)
                q_out(b, 0)
                decay_out(b, 0)
                decay_out(b, 1)
                q_out(b, 1)
                gamma_out(b)
                g_out(b, 0)
                g_out(b, 1)
                g_out(b, 2)
                split_hi(b + 1, raw, GLA)
                g_out(b, 3)

            def conv(b):
                for j in range(4):
                    wait_tile(act, CONV, b, 4 * j)
                    if not (is_first(b) and j == 0):
                        act.wait_ge(conv_step, 7 * (4 * b + j - 1) + C_U)
                    nc.scalar.activation(ccs[:], ps[TURN[(4 * j) % 8]][:], ACT.Copy).then_inc(cc_copied, 1)
                    if is_first(b) and j == 0:
                        head_squares(NB - 1, 0)
                        head_rms(NB - 1, 0)
                        head_squares(NB - 1, 1)
                        head_rms(NB - 1, 1)
                    if is_first(b) and j == 1:
                        head_rms(NB - 1, 2)
                        head_squares(NB - 1, 3)
                        head_rms(NB - 1, 3)
                    wait_tile(act, CONV, b, 4 * j + 2)
                    if not (is_first(b) and j == 0):
                        act.wait_ge(conv_step, 7 * (4 * b + j - 1) + C_DONE)
                    nc.scalar.activation(sgc[:], ps[TURN[(4 * j + 2) % 8]][:], ACT.Silu).then_inc(silu_ready, 1)
                    if is_first(b) and j == 0:
                        head_squares(NB - 1, 2)
                split_hi(NB + b + 1, raw, OUT if is_last(b) else CONV)

            def out_proj(b):
                if is_last(b):
                    split_p_hi(0)
                split_hi(2 * NB + b + 1, raw, OUT)

            def split_p_hi(b):
                act.wait_ge(p_loaded, 16 * (b + 1))
                if not is_first(b):
                    wait_tile(act, GATE, b - 1, TILES[GATE] - 2)
                for k in range(PLE_K):
                    nc.scalar.activation(PH[:, k], p_raw[:, k], ACT.Copy).then_inc(p_hi, 1)

            def gate(b, odd=0):
                for m in range(KT):
                    if m == KT - 1 and not is_last(b):
                        split_p_hi(b + 1)
                        split_hi(3 * NB + b + 1, raws[1 - odd], GATE)
                    wait_tile(act, GATE, b, 2 * m + 1)
                    if not (is_first(b) and m < 2):
                        act.wait_ge(gated, 8 * b + m - 1)
                    nc.scalar.activation(gt[:, m % 2], ps[m % 3][:], ACT.Sigmoid,
                                         bias=vec[:, V_BG + m:V_BG + m + 1]).then_inc(gate_ready, 1)
                    if m == 0 and not is_first(b):
                        out_rms(b - 1)
                    act.wait_ge(mixed, 8 * b + m + 1)
                    if not (is_first(b) and m < 2):
                        act.wait_ge(out_sum, 8 * b + m - 1)
                    nc.scalar.activation(osq[:, m % 2], raws[odd][:, m], ACT.Square).then_inc(out_sq, 1)

            def out_rms(b):
                act.wait_ge(out_mean, b + 1)
                nc.scalar.activation(R[:], ps[STAT][:], ACT.Sqrt, bias=eps[:], scale=1.0 / D_MODEL).then_inc(
                    out_root, 1)

            act.wait_ge(memsets, 3)
            act.wait_ge(consts_loaded, 64)
            x_squares(0, range(KT))
            x_rms(0)
            split_hi(0, raw, GLA)
            over_blocks(act, gla, apart=2)
            over_blocks(act, conv)
            over_blocks(act, out_proj)
            for c in range(2):
                act.wait_ge(y_stored[c], 16 * 4 * NB)
            over_blocks(act, gate, pair=True)
            out_rms(NB - 1)

        @block.vector
        def _(dve):
            def split_lo(step, src):
                for k in range(KT):
                    dve.wait_ge(x_hi, 8 * step + k + 1)
                    nc.vector.tensor_tensor(XL[:, k], src[:, k], XH[:, k].bitcast(F32), ALU.subtract).then_inc(
                        x_lo, 1)

            def x_sums(s, ks):
                for k in ks:
                    dve.wait_ge(x_sq, 8 * s + k + 1)
                    if k == 0:
                        if not is_first(s):
                            dve.wait_ge(n_ready, 8 * s)
                            dve.wait_ge(r_stored, 16 * s)
                        nc.vector.tensor_copy(R[:], sqs[0]).then_inc(x_sum, 1)
                    else:
                        dve.wait_ge(x_sum, 8 * s + k)
                        nc.vector.tensor_tensor(R[:], R[:], sqs[k % 4], ALU.add).then_inc(x_sum, 1)

            def x_recip(s):
                dve.wait_ge(x_root, s + 1)
                nc.vector.reciprocal(R[:], R[:]).then_inc(x_rstd, 1)

            def normalise(step, ks):
                for k in ks:
                    if k % 2 == 0:
                        dve.wait_ge(raw_loaded[k // 2], 16 * (step + 1))
                    nc.vector.scalar_tensor_tensor(out=raw[:, k], in0=raw[:, k],
                                                   scalar=vec[:, V_NORM + k:V_NORM + k + 1], in1=R[:],
                                                   op0=ALU.mult, op1=ALU.mult).then_inc(n_ready, 1)

            def head(b, h):
                n = 4 * b + h
                dve.wait_ge(head_root, n + 1)
                nc.vector.reciprocal(rt[:], rt[:]).then_inc(head_step, 1)
                dve.wait_ge(head_step, 3 * n + H_RECIP)
                if not (is_first(b) and h < 2):
                    dve.wait_ge(y_stored[h % 2], 16 * (2 * b + h // 2))
                nc.vector.scalar_tensor_tensor(out=y_sb[:, h % 2], in0=ps[O_BANK[h % 2]][:],
                                               scalar=vec[:, V_GLA:V_GLA + 1], in1=rt[:],
                                               op0=ALU.mult, op1=ALU.mult).then_inc(head_step, 1)
                dve.wait_ge(head_step, 3 * n + H_SCALED)
                dve.wait_ge(evacuated, 14 * b + 11 + h)
                nc.vector.tensor_tensor(y_sb[:, h % 2], y_sb[:, h % 2], sg[:, h], ALU.mult).then_inc(head_step, 1)

            def add_bias(b, i):
                dve.wait_ge(z_done, 2 * b + i + 1)
                if i == 0 and not is_first(b):
                    dve.wait_ge(gm_done, b)
                nc.vector.tensor_tensor(L[:, 2 * i:2 * i + 2].rearrange("p t c -> p (t c)"), ps[SMALL][:],
                                        bias2[:], ALU.add).then_inc(z_ready, 1)

            def minus_abs(b):
                dve.wait_ge(z_ready, 2 * b + 2)
                if not is_last(b):
                    dve.wait_ge(x_sum, 8 * (b + 2))
                dve.wait_ge(kdec, 2 * b) if not is_first(b) else None
                z = L[:].rearrange("p t c -> p (t c)")
                nc.vector.scalar_tensor_tensor(out=tmp[:].rearrange("p i c -> p (i c)"), in0=z, scalar=-1.0,
                                               in1=z, op0=ALU.mult, op1=ALU.min).then_inc(z_neg, 1)

            def log_decay(b):
                dve.wait_ge(z_log, b + 1)
                z = L[:].rearrange("p t c -> p (t c)")
                nc.vector.scalar_tensor_tensor(out=z, in0=z, scalar=0.0,
                                               in1=tmp[:].rearrange("p i c -> p (i c)"),
                                               op0=ALU.min, op1=ALU.subtract).then_inc(loga, 1)

            def decay_k(b, i):
                dve.wait_ge(decay, 2 * b + i + 1)
                k = ka_sb[:, 2 * i:2 * i + 2, 0:QK]
                nc.vector.tensor_tensor(k, k, tmp[:, i].rearrange("p (t c) -> p t c", t=2), ALU.mult).then_inc(
                    kdec, 1)

            def state(b, ch):
                dve.wait_ge(ds_done, NCH * b + ch + 1)
                if ch == 0:
                    dve.wait_ge(gamma_ready, b + 1)
                    if not is_first(b):
                        dve.wait_ge(o_done, HEADS * b)
                if not (is_first(b) and ch == 0):
                    dve.wait_ge(s_updated, 2 * (NCH * b + ch))
                for f in range(2):
                    nc.vector.scalar_tensor_tensor(out=hist[:, ch, f], in0=hist[:, (ch - 1) % NCH, f],
                                                   scalar=gamma[:, f, ch:ch + 1],
                                                   in1=ps[DS_BANK[ch % 2]][:, f * DV:f * DV + DV],
                                                   op0=ALU.mult, op1=ALU.add).then_inc(s_updated, 1)

            def gla(b):
                tail = not is_first(b)
                nxt = not is_last(b)
                if tail:
                    head(b - 1, 0)
                    head(b - 1, 1)
                    head(b - 1, 2)
                if nxt:
                    x_sums(b + 1, range(0, 4))
                if tail:
                    head(b - 1, 3)
                if nxt:
                    x_sums(b + 1, range(4, 8))
                add_bias(b, 0)
                if nxt:
                    x_recip(b + 1)
                add_bias(b, 1)
                minus_abs(b)
                if nxt:
                    dve.wait_ge(x_rstd, b + 2)
                else:
                    dve.wait_ge(r_loaded, 16)
                normalise(b + 1, range(0, 4))
                log_decay(b)
                normalise(b + 1, range(4, 8))
                decay_k(b, 0)
                decay_k(b, 1)
                for ch in range(NCH):
                    state(b, ch)
                split_lo(b + 1, raw)

            def conv(b):
                for j in range(4):
                    n = 4 * b + j
                    if not is_first(b):
                        dve.wait_ge(conv_step, 7 * (n - 4) + C_W2)
                        nc.vector.tensor_copy(u[:, j, 0:2], u[:, j, TB:TB + 2]).then_inc(conv_step, 1)
                    else:
                        nc.vector.memset(u[:, j, 0:2], 0.0).then_inc(conv_step, 1)
                    dve.wait_ge(conv_step, 7 * n + C_CARRY)
                    wait_tile(dve, CONV, b, 4 * j + 1)
                    dve.wait_ge(cc_copied, n + 1)
                    nc.vector.tensor_tensor(u[:, j, 2:2 + TB], ccs[:], ps[TURN[(4 * j + 1) % 8]][:],
                                            ALU.mult).then_inc(conv_step, 1)
                    dve.wait_ge(conv_step, 7 * n + C_U)
                    w = V_CW + 3 * j
                    nc.vector.tensor_scalar(cv[:], u[:, j, 0:TB], vec[:, w:w + 1],
                                            vec[:, V_CB + j:V_CB + j + 1], ALU.mult, ALU.add).then_inc(conv_step, 1)
                    for i in (1, 2):
                        dve.wait_ge(conv_step, 7 * n + C_W0 + i - 1)
                        nc.vector.scalar_tensor_tensor(out=cv[:], in0=u[:, j, i:i + TB],
                                                       scalar=vec[:, w + i:w + i + 1], in1=cv[:],
                                                       op0=ALU.mult, op1=ALU.add).then_inc(conv_step, 1)
                    if is_first(b) and j == 0:
                        head(NB - 1, 0)
                        head(NB - 1, 1)
                    if j == 3:
                        split_lo(NB + b + 1, raw)
                    wait_tile(dve, CONV, b, 4 * j + 3)
                    dve.wait_ge(conv_step, 7 * n + C_W2)
                    nc.vector.tensor_tensor(cv[:], cv[:], ps[TURN[(4 * j + 3) % 8]][:], ALU.mult).then_inc(
                        conv_step, 1)
                    if is_first(b) and j == 0:
                        head(NB - 1, 2)
                        head(NB - 1, 3)
                    dve.wait_ge(conv_step, 7 * n + C_GATED)
                    dve.wait_ge(silu_ready, n + 1)
                    dve.wait_ge(y_stored[j % 2], 16 * (2 * NB + 2 * b + j // 2))
                    nc.vector.tensor_tensor(y_sb[:, j % 2], cv[:], sgc[:], ALU.mult).then_inc(conv_step, 1)
                    if j == 1 and not is_last(b):
                        dve.wait_ge(r_loaded, 16 * (b + 2))
                        normalise(NB + b + 1, range(KT))

            def out_proj(b):
                for m in range(KT):
                    if m == KT - 1:
                        if is_last(b):
                            split_p_lo(0)
                        split_lo(2 * NB + b + 1, raw)
                    wait_tile(dve, OUT, b, m)
                    dve.wait_ge(xt_loaded[m % 4], 16 * (2 * b + m // 4 + 1))
                    nc.vector.tensor_tensor(xt[:, m % 4], xt[:, m % 4], ps[TURN[m]][:], ALU.add).then_inc(
                        h_ready, 1)

            def split_p_lo(b):
                dve.wait_ge(p_hi, 2 * (b + 1))
                for k in range(PLE_K):
                    nc.vector.tensor_tensor(PL[:, k], p_raw[:, k], PH[:, k].bitcast(F32), ALU.subtract).then_inc(
                        p_lo, 1)

            def gate(b, odd=0):
                def add_square(m):
                    dve.wait_ge(out_sq, 8 * b + m + 1)
                    if m == 0:
                        if is_first(b):
                            for c in range(4):
                                dve.wait_ge(h_stored[c], 16 * 2 * NB)
                        else:
                            dve.wait_ge(out_mean, b)
                        nc.vector.tensor_copy(acc[:], osq[:, 0]).then_inc(out_sum, 1)
                    else:
                        dve.wait_ge(out_sum, 8 * b + m)
                        nc.vector.tensor_tensor(acc[:], acc[:], osq[:, m % 2], ALU.add).then_inc(out_sum, 1)

                for m in range(KT):
                    if m == KT - 1 and not is_last(b):
                        split_p_lo(b + 1)
                        split_lo(3 * NB + b + 1, raws[1 - odd])
                    wait_tile(dve, GATE, b, 2 * m)
                    dve.wait_ge(gate_ready, 8 * b + m + 1)
                    if not (is_first(b) and m == 0):
                        dve.wait_ge(mixed, 8 * b + m)
                    nc.vector.tensor_tensor(t_sb[:], gt[:, m % 2], ps[3 + m % 3][:], ALU.mult).then_inc(gated, 1)
                    dve.wait_ge(gated, 8 * b + m + 1)
                    nc.vector.tensor_tensor(raws[odd][:, m], raws[odd][:, m], t_sb[:], ALU.add).then_inc(mixed, 1)
                    if m >= 1:
                        add_square(m - 1)
                    if m == 0 and not is_first(b):
                        final_norm(b - 1, 1 - odd)
                add_square(KT - 1)

            def final_norm(b, odd):
                dve.wait_ge(out_root, b + 1)
                nc.vector.reciprocal(R[:], R[:]).then_inc(out_rstd, 1)
                dve.wait_ge(out_rstd, b + 1)
                for m in range(KT):
                    nc.vector.scalar_tensor_tensor(out=raws[odd][:, m], in0=raws[odd][:, m],
                                                   scalar=vec[:, V_FIN + m:V_FIN + m + 1], in1=R[:],
                                                   op0=ALU.mult, op1=ALU.mult).then_inc(out_norm, 1)

            dve.wait_ge(memsets, 3)
            dve.wait_ge(consts_loaded, 64)
            x_sums(0, range(KT))
            x_recip(0)
            dve.wait_ge(x_rstd, 1)
            normalise(0, range(KT))
            split_lo(0, raw)
            over_blocks(dve, gla, apart=2)
            over_blocks(dve, conv)
            over_blocks(dve, out_proj)
            over_blocks(dve, gate, pair=True)
            final_norm(NB - 1, 1)


def kernel(x, p, norm_w, w_in, w_alpha_up, b_alpha, gla_norm_w, conv_w, conv_b,
           w_out, w_ple, w_ple_gate, b_ple_gate, final_norm_w):
    import numpy as np
    import concourse.bacc as bacc
    from concourse.bass_utils import run_bass_kernel_spmd

    def blocks(a):
        return np.ascontiguousarray(np.asarray(a).reshape(NB, TB, -1, P).transpose(0, 3, 2, 1))

    def tiles(w):
        w = np.asarray(w)
        return np.ascontiguousarray(w.reshape(w.shape[0] // P, P, -1, P).transpose(2, 1, 0, 3)).reshape(
            w.shape[1] // P, P, -1)

    def cols(v):
        return np.asarray(v).reshape(-1, P).T

    w = np.asarray(w_in)[0]
    q, k, v, g, a, cb, cc, cu, gc = np.split(w, np.cumsum([256, 256, 512, 512, 16, 512, 512, 512]), axis=1)
    ka = np.concatenate([k, a], axis=1).reshape(KT, P, KA).transpose(1, 0, 2)
    conv = np.stack([m.reshape(D_MODEL, 4, P) for m in (cc, cu, gc, cb)], axis=2).reshape(D_MODEL, 4 * 512)
    ple = np.asarray(w_ple)[0].reshape(PLE_K, P, D_MODEL)

    r = np.arange(P)
    same = (r[:, None] // CHUNK) == (r[None, :] // CHUNK)
    tau = 16.0
    masks = np.concatenate([(same & (r[:, None] > r[None, :])) / tau, np.eye(P),
                            ((r[:, None] // CHUNK) == np.arange(2)[None, :]) / tau], axis=1).astype(np.float32)
    cw = np.asarray(conv_w)[0].reshape(3, 4, P).transpose(2, 1, 0).reshape(P, 12)
    vectors = np.concatenate([cols(np.asarray(norm_w)[0]), cols(np.asarray(gla_norm_w)[0]), cw,
                              cols(np.asarray(conv_b)[0]), cols(np.asarray(b_ple_gate)[0]),
                              cols(final_norm_w)], axis=1)
    ba = np.asarray(b_alpha)[0]
    arrays = {
        "xb": blocks(np.asarray(x)[0]), "pb": blocks(np.asarray(p)[0, 0]), "w_ka": ka,
        "w_in": tiles(np.concatenate([v, q, g, conv], axis=1)), "w_out": tiles(np.asarray(w_out)[0]),
        "w_gate": tiles(np.asarray(w_ple_gate)[0]), "w_ple": ple, "w_up": np.asarray(w_alpha_up)[0],
        "b_alpha": np.broadcast_to(np.concatenate([ba, ba]), (P, 2 * QK)), "vectors": vectors, "masks": masks,
    }
    arrays = {f"{n}_dram": np.ascontiguousarray(a) for n, a in arrays.items()}

    nc = bacc.Bacc("TRN2", target_bir_lowering=False, num_devices=1, dynamic_dma_scratch_size=2048)
    args = [nc.dram_tensor(n, a.shape, F32, kind="ExternalInput").ap() for n, a in arrays.items()]
    args.append(nc.dram_tensor("out_dram", (NB, P, KT, TB), F32, kind="ExternalOutput").ap())
    args.append(nc.dram_tensor("y_scratch", (NB, P, KT, TB), F32).ap())
    args.append(nc.dram_tensor("h_scratch", (NB, P, KT, TB), F32).ap())
    args.append(nc.dram_tensor("r_scratch", (NB, P, TB), F32).ap())
    build(nc, *args)
    res = run_bass_kernel_spmd(nc, [arrays], core_ids=[0])
    o = res.results[0]["out_dram"]
    return o.transpose(0, 3, 2, 1).reshape(1, SEQ, D_MODEL)
```

```python
from contextlib import ExitStack

import concourse.bass as bass
from concourse import mybir

P = 128
D_MODEL, SEQ = 1024, 4096
TB = 512
NB = SEQ // TB
KT = D_MODEL // P
HEADS, DK, DV = 4, 64, 128
QK, RANK, CHUNK = HEADS * DK, 16, 64
KA = QK + RANK
TT = TB // P
NCH = TB // CHUNK
PLE_K = 2
EPS = 1e-6
FIRST_LO = 3
SLOTS = 16
BIG = D_MODEL * 4

F32 = mybir.dt.float32
F32R = mybir.dt.float32r
ACT = mybir.ActivationFunctionType
ALU = mybir.AluOpType

GLA, CONV, OUT, GATE = range(4)

V_NORM, V_GLA, V_CW, V_CB, V_BG, V_FIN = 0, 8, 9, 21, 25, 33
N_VEC = 41

W_KA, W_V, W_Q, W_G, W_CONV, W_OUT, W_GATE, W_PLE, N_W = 0, 4, 8, 10, 14, 30, 38, 46, 48
KA_SLOT = 10
RING_ORDER = [10, 11, 12, 0, 1, 2, 3, 4, 5, 6, 7, 8, 9, 13, 14, 15]


def slot_of(n):
    if n < W_CONV:
        return n - W_V
    if n < W_OUT:
        return RING_ORDER[n - W_CONV]
    if n < W_PLE:
        return RING_ORDER[n - W_OUT]
    return RING_ORDER[n - W_PLE]


MAIN = (0, 1, 2)
O_BANK = (3, 4)
DS_BANK = (5, 6)
SMALL = 7
TURN = (0, 1, 2, 5, 6, 3, 4, 7)
STAT = 6

H_RECIP, H_SCALED, H_DONE = 1, 2, 3
C_CARRY, C_U, C_W0, C_W1, C_W2, C_GATED, C_DONE = range(1, 8)
TILES = {GLA: 14, CONV: 16, OUT: 8, GATE: 16}


def build(nc, xb, pb, w_ka, w_in, w_out, w_gate, w_ple, w_up, b_alpha, vectors, masks,
          out, y_scratch, h_scratch, r_scratch):
    with ExitStack() as ctx:
        def sb(name, shape, dt=F32):
            return ctx.enter_context(nc.sbuf_tensor(name, shape, dt))

        def sem(name):
            return ctx.enter_context(nc.semaphore(name))

        def over(name, shape, at, dt=F32):
            return nc.alloc_sbuf_tensor_at(name, shape, dt, offset=at)

        ps = [ctx.enter_context(nc.psum_tensor(f"bank{i}", [P, 512], F32)) for i in range(8)]

        wh_at = (nc.sbuf_base + 31) // 32 * 32
        WH = sb("WH", [P, SLOTS, KT, P], F32R)
        wl_at = wh_at + SLOTS * BIG
        WL = sb("WL", [P, SLOTS, KT, P], F32R)
        XH = sb("XH", [P, KT, TB], F32R)
        XL = sb("XL", [P, KT, TB], F32R)
        raw = sb("raw", [P, KT, TB])
        stage = sb("stage", [P, 2, D_MODEL])
        vec = sb("vec", [P, N_VEC])
        eps = sb("eps", [P, 1])
        warm = sb("warm", [P, 1])
        mask = sb("mask", [P, P + 2])
        ones = sb("ones", [P, P])
        y_sb = sb("y_sb", [P, 2, TB])
        R = sb("R", [P, TB])
        suffix, member = mask[:, 0:P], mask[:, P:P + 2]

        KAH = WH[:, KA_SLOT:KA_SLOT + 3].rearrange("p s k c -> p (s k c)")[:, 0:KT * KA].rearrange(
            "p (k c) -> p k c", k=KT)
        KAL = WL[:, KA_SLOT:KA_SLOT + 3].rearrange("p s k c -> p (s k c)")[:, 0:KT * KA].rearrange(
            "p (k c) -> p k c", k=KT)
        tail_at = wh_at + KA_SLOT * BIG + KT * KA * 4
        ident = over("ident", [P, P], tail_at)
        bias2 = over("bias2", [P, 2 * QK], tail_at + P * 4)
        wup = over("wup", [RANK, QK], tail_at + (P + 2 * QK) * 4)
        v_sb = over("v_sb", [P, TT, HEADS * DV], wh_at + 13 * BIG)
        hist = over("hist", [P, NCH, 2, DV], wl_at + 13 * BIG)
        L = over("L", [P, TT, QK], wh_at + 15 * BIG)
        q_diag = [over("q_diag0", [P, NCH, 2, CHUNK], wl_at + 15 * BIG), sb("q_diag1", [P, NCH, 2, CHUNK])]
        raw_odd = over("raw_odd", [P, KT, TB], wh_at)
        raws = (raw, raw_odd)

        ROW = TB * 4
        a_at = (nc.sbuf_base + 31) // 32 * 32
        region_a = sb("region_a", [P, 14592 // 4])
        ka_sb = over("ka_sb", [P, TT, KA], a_at)
        aT = over("aT", [RANK, TB], a_at + 4352)
        tmp = over("tmp", [P, 2, TB], a_at + 4352 + ROW)
        sq = over("sq", [P, 2, TB], a_at + 4352 + 3 * ROW)
        u = over("u", [P, 4, 2 + TB], a_at)
        ccs = over("ccs", [P, TB], a_at + 8224)
        cv = over("cv", [P, TB], a_at + 8224 + ROW)
        sgc = over("sgc", [P, TB], a_at + 8224 + 2 * ROW)
        p_raw = over("p_raw", [P, PLE_K, TB], a_at)
        PH = over("PH", [P, PLE_K, TB], a_at + 2 * ROW, F32R)
        PL = over("PL", [P, PLE_K, TB], a_at + 4 * ROW, F32R)
        t_sb = over("t_sb", [P, TB], a_at + 6 * ROW)
        b_at = (nc.sbuf_base + 31) // 32 * 32
        region_b = sb("region_b", [P, 12288 // 4])
        sg = over("sg", [P, HEADS, TB], b_at)
        hsq = over("hsq", [P, TB], b_at + 4 * ROW)
        rt = over("rt", [P, TB], b_at + 5 * ROW)
        xt = over("xt", [P, 4, TB], b_at)
        acc = over("acc", [P, TB], b_at)
        gt = over("gt", [P, 2, TB], b_at + 4 * ROW)
        osq = y_sb
        early_ka = [L[:].rearrange("p t c -> p (t c)"), tmp[:].rearrange("p i c -> p (i c)")]
        early_v3 = over("early_v3", [P, 3, D_MODEL], b_at)
        early_v = [early_v3[:, 0], early_v3[:, 1], early_v3[:, 2], y_sb[:].rearrange("p i c -> p (i c)")]
        gamma = sb("gamma", [P, 2, NCH])

        consts_loaded = sem("consts_loaded")
        memsets = sem("memsets")
        stage_loaded = [sem(f"stage_loaded{i}") for i in range(2)]
        early_loaded = [sem(f"early_loaded{i}") for i in range(6)]
        w_hi = sem("w_hi")
        w_ready = sem("w_ready")
        raw_loaded = [sem(f"raw_loaded{i}") for i in range(4)]
        n_ready = sem("n_ready")
        x_hi = sem("x_hi")
        x_lo = sem("x_lo")
        x_free = sem("x_free")
        tile_done = [sem(f"tile_done_{n}") for n in ("gla", "conv", "out", "gate")]
        x_sq = sem("x_sq")
        x_sum = sem("x_sum")
        x_mean = sem("x_mean")
        x_root = sem("x_root")
        x_rstd = sem("x_rstd")
        r_stored = sem("r_stored")
        r_loaded = sem("r_loaded")
        evacuated = sem("evacuated")
        aT_done = sem("aT_done")
        aT_ready = sem("aT_ready")
        z_done = sem("z_done")
        z_ready = sem("z_ready")
        z_neg = sem("z_neg")
        z_exp = sem("z_exp")
        z_log = sem("z_log")
        loga = sem("loga")
        cum_done = sem("cum_done")
        decay = sem("decay")
        kdec = sem("kdec")
        gm_done = sem("gm_done")
        gamma_ready = sem("gamma_ready")
        ds_done = sem("ds_done")
        s_updated = sem("s_updated")
        o_done = sem("o_done")
        head_sq = sem("head_sq")
        head_mean = sem("head_mean")
        head_root = sem("head_root")
        head_step = sem("head_step")
        y_stored = [sem(f"y_stored{i}") for i in range(2)]
        cc_copied = sem("cc_copied")
        silu_ready = sem("silu_ready")
        conv_step = sem("conv_step")
        xt_loaded = [sem(f"xt_loaded{i}") for i in range(4)]
        h_ready = sem("h_ready")
        h_stored = [sem(f"h_stored{i}") for i in range(4)]
        p_loaded = sem("p_loaded")
        p_hi = sem("p_hi")
        p_lo = sem("p_lo")
        gate_ready = sem("gate_ready")
        gated = sem("gated")
        mixed = sem("mixed")
        out_sq = sem("out_sq")
        out_sum = sem("out_sum")
        out_mean = sem("out_mean")
        out_root = sem("out_root")
        out_rstd = sem("out_rstd")
        out_norm = sem("out_norm")
        out_stored = [sem(f"out_stored{i}") for i in range(4)]

        def wait_tile(eng, phase, b, i):
            if i == TILES[phase] - 1:
                eng.wait_ge(x_free, 8 * (8 * phase + b + 1))
            else:
                eng.wait_ge(tile_done[phase], (TILES[phase] - 1) * b + i + 1)

        def over_blocks(eng, body, pair=False, apart=1):
            for b in range(apart):
                body(b)
            if pair:
                with eng.Fori(1, NB - 2, 2) as b:
                    body(b, 1)
                    body(b + 1, 0)
            else:
                with eng.Fori(apart, NB - 1) as b:
                    body(b)
            body(NB - 1, 1) if pair else body(NB - 1)

        def is_first(b):
            return isinstance(b, int) and b == 0

        def is_last(b):
            return isinstance(b, int) and b == NB - 1

        block = ctx.enter_context(nc.Block())

        @block.sync
        def _(sp):
            def load_raw(dst, src, step):
                for c in range(4):
                    sp.dma_start(dst[:, 2 * c:2 * c + 2], src[:, 2 * c:2 * c + 2]).then_inc(raw_loaded[c], 16)

            def store_y(n, b, k):
                sp.dma_start(y_scratch[b, :, k], y_sb[:, k % 2]).then_inc(y_stored[k % 2], 16)

            def store_r(b):
                sp.wait_ge(x_rstd, b + 1)
                sp.dma_start(r_scratch[b], R[:]).then_inc(r_stored, 16)

            def store_heads(b):
                for h in range(HEADS):
                    sp.wait_ge(head_step, 3 * (4 * b + h) + H_DONE)
                    tokens = slice(h % 2 * TB // 2, (h % 2 + 1) * TB // 2)
                    sp.dma_start(y_scratch[b, :, h // 2 * 2:h // 2 * 2 + 2, tokens],
                                 y_sb[:, h % 2].rearrange("p (h t) -> p h t", h=2)).then_inc(y_stored[h % 2], 16)

            def gla(b):
                sp.wait_ge(x_lo, 8 * (b + 1))
                load_raw(raw, xb[0] if is_last(b) else xb[b + 1], b + 1)
                if not is_first(b):
                    store_heads(b - 1)
                if is_last(b):
                    sp.wait_ge(r_stored, 16 * NB)
                    sp.wait_ge(n_ready, 8 * NB)
                    sp.dma_start(R[:], r_scratch[0]).then_inc(r_loaded, 16)
                else:
                    store_r(b + 1)

            def conv(b):
                sp.wait_ge(x_lo, 8 * (NB + b + 1))
                if is_last(b):
                    sp.wait_ge(y_stored[0], 16 * (2 * NB + 2 * (NB - 1)))
                    sp.wait_ge(y_stored[1], 16 * (2 * NB + 2 * (NB - 1)))
                    load_raw(raw, y_scratch[0], 2 * NB)
                else:
                    load_raw(raw, xb[b + 1], NB + b + 1)
                    sp.wait_ge(n_ready, 8 * (NB + b + 1))
                    sp.dma_start(R[:], r_scratch[b + 1]).then_inc(r_loaded, 16)
                if is_first(b):
                    store_heads(NB - 1)
                for j in range(4):
                    sp.wait_ge(conv_step, 7 * (4 * b + j) + C_DONE)
                    store_y(4 * NB + 4 * b + j, b, 4 + j)

            def load_xt(b, m):
                sp.dma_start(xt[:, m % 4], xb[b, :, m]).then_inc(xt_loaded[m % 4], 16)

            def out_proj(b):
                sp.wait_ge(x_lo, 8 * (2 * NB + b + 1))
                if is_last(b):
                    for c in range(4):
                        sp.wait_ge(h_stored[c], 16 * 2 * (NB - 1))
                    load_raw(raw, h_scratch[0], 3 * NB)
                    sp.dma_start(p_raw[:], pb[0]).then_inc(p_loaded, 16)
                else:
                    for c in range(2):
                        sp.wait_ge(y_stored[c], 16 * 4 * NB)
                    load_raw(raw, y_scratch[b + 1], 2 * NB + b + 1)
                for m in range(KT):
                    sp.wait_ge(h_ready, 8 * b + m + 1)
                    sp.dma_start(h_scratch[b, :, m], xt[:, m % 4]).then_inc(h_stored[m % 4], 16)
                    if is_last(b) and m + 2 >= KT:
                        continue
                    if not is_first(b) or m >= 2:
                        sp.wait_ge(h_stored[(m + 2) % 4], 16 * (2 * b + (m + 2) // 4))
                    if m + 2 < KT:
                        load_xt(b, m + 2)
                    else:
                        load_xt(b + 1, m + 2 - KT)

            def store_out(b, odd):
                for c in range(4):
                    sp.wait_ge(out_norm, 8 * b + 2 * c + 2)
                    sp.dma_start(out[b, :, 2 * c:2 * c + 2], raws[odd][:, 2 * c:2 * c + 2]).then_inc(
                        out_stored[c], 16)

            def gate(b, odd=0):
                if not is_last(b):
                    sp.wait_ge(p_lo, 2 * (b + 1))
                    sp.dma_start(p_raw[:], pb[b + 1]).then_inc(p_loaded, 16)
                if is_first(b):
                    sp.wait_ge(x_free, 8 * 3 * NB)
                    for c in range(4):
                        sp.wait_ge(h_stored[c], 16 * 2 * NB)
                else:
                    store_out(b - 1, 1 - odd)
                if not is_last(b):
                    if not is_first(b):
                        for c in range(4):
                            sp.wait_ge(out_stored[c], 16 * b)
                    load_raw(raws[1 - odd], h_scratch[b + 1], 3 * NB + b + 1)

            load_raw(raw, xb[0], 0)
            for i in range(2):
                sp.dma_start(early_ka[i][:, 0:2 * KA], w_ka[:, 4 + 2 * i:6 + 2 * i].rearrange("p k c -> p (k c)")).then_inc(
                    early_loaded[i], 16)
            sp.dma_start(vec[:], vectors).then_inc(consts_loaded, 16)
            sp.dma_start(mask[:], masks[:, 0:P + 2]).then_inc(consts_loaded, 16)
            sp.dma_start(ident[:], masks[:, P + 2:]).then_inc(consts_loaded, 16)
            sp.dma_start(bias2[:], b_alpha).then_inc(consts_loaded, 16)
            sp.dma_start(wup[:], w_up).then_inc(consts_loaded, 16)
            for i in range(4):
                sp.dma_start(early_v[i], w_in[i]).then_inc(early_loaded[2 + i], 16)
            store_r(0)
            over_blocks(sp, gla, apart=2)
            over_blocks(sp, conv)
            load_xt(0, 0)
            load_xt(0, 1)
            over_blocks(sp, out_proj)
            over_blocks(sp, gate, pair=True)
            store_out(NB - 1, 1)
            for c in range(4):
                sp.wait_ge(out_stored[c], 16 * NB)

        @block.gpsimd
        def _(pool):
            pool.memset(ones[:], 1.0).then_inc(memsets, 1)
            pool.memset(eps[:], EPS).then_inc(memsets, 1)
            pool.memset(hist[:, NCH - 1], 0.0).then_inc(memsets, 1)
            for pair in range(2):
                pool.memset(q_diag[pair][:], 0.0).then_inc(memsets, 1)

            def source(n):
                if n < W_V:
                    return w_ka[:, 2 * n:2 * n + 2].rearrange("p k c -> p (k c)")
                if n < W_OUT:
                    return w_in[n - W_V]
                if n < W_GATE:
                    return w_out[n - W_OUT]
                if n < W_PLE:
                    return w_gate[n - W_GATE]
                return w_ple[n - W_PLE]

            def load(n):
                if n >= W_Q + 2:
                    pool.wait_ge(w_ready, n - 1)
                src = source(n)
                pool.dma_start(stage[:, n % 2, 0:src.shape[1]], src).then_inc(stage_loaded[n % 2], 16)

            def wait_slot_free(n):
                if n < W_CONV:
                    return
                if n < W_OUT:
                    s = slot_of(n)
                    if s >= 13:
                        pool.wait_ge(o_done, HEADS * NB)
                    elif s == KA_SLOT + 2:
                        pool.wait_ge(z_ready, 2 * NB)
                    elif s >= KA_SLOT:
                        wait_tile(pool, GLA, NB - 1, 3)
                    elif s < 4:
                        wait_tile(pool, GLA, NB - 1, 7)
                    else:
                        wait_tile(pool, GLA, NB - 1, 4 + s)
                elif n < W_PLE:
                    wait_tile(pool, CONV, NB - 1, n - W_OUT)
                else:
                    wait_tile(pool, OUT, NB - 1, n - W_PLE)

            def x_sums(s):
                for k in range(1, KT):
                    pool.wait_ge(x_sq, 8 * s + k + 1)
                    if k == 1:
                        pool.wait_ge(n_ready, 8 * s)
                        pool.wait_ge(r_stored, 16 * s)
                    else:
                        pool.wait_ge(x_sum, 7 * s + k - 1)
                    pool.tensor_tensor(R[:], sq[:, 0] if k == 1 else R[:], sq[:, k % 2], ALU.add).then_inc(
                        x_sum, 1)

            def lo_of_block_0():
                for k in range(FIRST_LO):
                    pool.wait_ge(x_hi, k + 1)
                    pool.tensor_tensor(XL[:, k], raw[:, k], XH[:, k].bitcast(F32), ALU.subtract).then_inc(x_lo, 1)

            load(0)
            load(1)
            for n in range(N_W):
                if n == W_CONV:
                    x_sums(2)
                    with pool.Fori(3, NB) as s:
                        x_sums(s)
                if n == W_V:
                    pool.wait_ge(w_ready, 2)
                    load(W_Q)
                    load(W_Q + 1)
                if W_Q < n < N_W - 1:
                    load(n + 1)
                if n == W_V:
                    lo_of_block_0()
                if 2 <= n < W_Q:
                    source_tile = early_ka[n - 2] if n < W_V else early_v[n - W_V]
                    pool.wait_ge(early_loaded[n - 2], 16)
                else:
                    source_tile = stage[:, n % 2]
                    pool.wait_ge(stage_loaded[n % 2], 16 * (n // 2 + 1 if n < 2 else n // 2 - 2))
                wait_slot_free(n)
                if n < W_V:
                    hi, lo = KAH[:, 2 * n:2 * n + 2], KAL[:, 2 * n:2 * n + 2]
                    src = source_tile[:, 0:2 * KA].rearrange("p (k c) -> p k c", k=2)
                else:
                    hi, lo = WH[:, slot_of(n)], WL[:, slot_of(n)]
                    src = source_tile.rearrange("p (k c) -> p k c", k=KT)
                pool.tensor_scalar(hi, src, 1.0, 0.0, ALU.mult, ALU.add).then_inc(w_hi, 1)
                pool.wait_ge(w_hi, n + 1)
                pool.tensor_tensor(lo, src, hi.bitcast(F32), ALU.subtract).then_inc(w_ready, 1)

        @block.tensor
        def _(pe):
            def big_tile(phase, b, i, acc_ap, products, after=None, waits=None):
                step = 8 * phase + b
                last = i == TILES[phase] - 1
                first = i == (1 if phase == GATE else 0)
                for k in range(KT):
                    hh, lh, hl = products(k)
                    if first:
                        pe.wait_ge(x_hi, 8 * step + k + 1)
                    nc.tensor.matmul(acc_ap, hh[0], hh[1], start=(k == 0), stop=False)
                    if lh[2]:
                        nc.tensor.matmul(acc_ap, lh[0], lh[1], start=False, stop=False)
                    if first:
                        pe.wait_ge(x_lo, 8 * step + k + 1)
                    if not lh[2]:
                        nc.tensor.matmul(acc_ap, lh[0], lh[1], start=False, stop=False)
                    if waits is not None:
                        waits(k)
                    mm = nc.tensor.matmul(acc_ap, hl[0], hl[1], start=False, stop=(k == KT - 1))
                    if last:
                        mm.then_inc(x_free, 1)
                    elif k == KT - 1:
                        mm.then_inc(tile_done[phase], 1)
                    if after is not None:
                        after(k)

            def halfway(small):
                return lambda k: small() if k == 3 else None

            def stationary_w(slot):
                return lambda k: ((WH[:, slot, k], XH[:, k], True), (WL[:, slot, k], XH[:, k], True),
                                  (WH[:, slot, k], XL[:, k], True))

            def weights(b, n):
                if is_first(b):
                    pe.wait_ge(w_ready, n + 1)

            def mean_of(bank, src):
                return nc.tensor.matmul(ps[bank][:], ones[:], src, start=True, stop=True)

            def x_stats(s):
                pe.wait_ge(x_sum, 7 * (s + 1))
                mean_of(SMALL, R[:]).then_inc(x_mean, 1)

            def main_bank(b, i):
                if i >= 3:
                    pe.wait_ge(evacuated, 14 * b + i - 2)
                elif not is_first(b):
                    pe.wait_ge(evacuated, 14 * b - (1, 0, 2)[i] if i != 2 else 14 * b - 2)
                return ps[MAIN[i % 3]]

            def ka_tile(b, t, after=None):
                if is_first(b):
                    pe.wait_ge(w_ready, W_V)
                tok = slice(t * P, t * P + P)
                big_tile(GLA, b, t, main_bank(b, t)[:, 0:KA],
                         lambda k: ((XH[:, k, tok], KAH[:, k], True), (XH[:, k, tok], KAL[:, k], True),
                                    (XL[:, k, tok], KAH[:, k], True)), after)

            def v_tile(b, t, after=None):
                if is_first(b):
                    pe.wait_ge(w_ready, W_Q)
                tok = slice(t * P, t * P + P)
                bank = main_bank(b, 4 + t)[:, :].rearrange("p (s c) -> p s c", s=4)
                big_tile(GLA, b, 4 + t, bank,
                         lambda k: ((XH[:, k, tok], WH[:, 0:4, k], True), (XH[:, k, tok], WL[:, 0:4, k], True),
                                    (XL[:, k, tok], WH[:, 0:4, k], True)), after)

            def gla_tile(b, i, n, after=None, waits=None):
                weights(b, n)
                big_tile(GLA, b, i, main_bank(b, i)[:], stationary_w(slot_of(n)), after, waits)

            def pair_out(b, pair, c):
                half = c // (NCH // 2)
                if c == 0 and pair == 0:
                    pe.wait_ge(s_updated, 2 * NCH * (b + 1))
                elif pair == 1 and c % (NCH // 2) == 0:
                    pe.wait_ge(head_step, 3 * (4 * b + half) + H_SCALED)
                bank = ps[O_BANK[half]][:].rearrange("p (h c t) -> p h c t", h=2, c=NCH // 2)
                mm = nc.tensor.matmul(bank[:, :, c % (NCH // 2)], hist[:, c, pair], q_diag[pair][:, c],
                                      start=True, stop=True)
                if c % (NCH // 2) == NCH // 2 - 1:
                    mm.then_inc(o_done, 1)

            def head_stat(b, h):
                if h == 0 and is_last(b):
                    pe.wait_ge(gamma_ready, b + 1)
                elif h == 0:
                    pe.wait_ge(x_root, b + 2)
                elif h == 2 and is_last(b):
                    pe.wait_ge(head_root, 4 * b + h)
                elif h == 2:
                    pe.wait_ge(z_ready, 2 * b + 4)
                else:
                    pe.wait_ge(head_root, 4 * b + h)
                pe.wait_ge(head_sq, 4 * b + h + 1)
                mean_of(SMALL, hsq[:]).then_inc(head_mean, 1)

            def turn_a(b):
                pe.wait_ge(evacuated, 14 * b + 4)
                if is_first(b):
                    pe.wait_ge(x_root, 1)
                else:
                    pe.wait_ge(head_root, 4 * (b - 1) + 2)
                for t in range(TT):
                    mm = nc.tensor.transpose(ps[SMALL][0:RANK, t * P:t * P + P], ka_sb[:, t, QK:KA], ident[:])
                mm.then_inc(aT_done, 1)

            def logits(b, i):
                for t in range(2 * i, 2 * i + 2):
                    mm = nc.tensor.matmul(ps[SMALL][:, (t % 2) * QK:(t % 2) * QK + QK],
                                          aT[:, t * P:t * P + P], wup[:], start=True, stop=True)
                mm.then_inc(z_done, 1)

            def suffix_sums(b, i):
                for t in range(2 * i, 2 * i + 2):
                    mm = nc.tensor.matmul(ps[SMALL][:, (t % 2) * QK:(t % 2) * QK + QK],
                                          suffix, L[:, t], start=True, stop=True)
                mm.then_inc(cum_done, 1)

            def chunk_sums(b):
                for f in range(2):
                    for t in range(TT):
                        mm = nc.tensor.matmul(ps[SMALL][:, f * NCH + 2 * t:f * NCH + 2 * t + 2],
                                              L[:, t, f * P:f * P + P], member, start=True, stop=True)
                mm.then_inc(gm_done, 1)

            def increments(b, c):
                for h in range(HEADS):
                    for ch in (c, c + 1):
                        rows = slice(CHUNK * (ch % 2), CHUNK * (ch % 2) + CHUNK)
                        mm = nc.tensor.matmul(
                            ps[DS_BANK[ch % 2]][DK * (h % 2):DK * (h % 2) + DK, (h // 2) * DV:(h // 2) * DV + DV],
                            ka_sb[rows, ch // 2, h * DK:h * DK + DK],
                            v_sb[rows, ch // 2, h * DV:h * DV + DV], start=True, stop=True)
                        if h == HEADS - 1:
                            mm.then_inc(ds_done, 1)

            def increment_waits(b, c):
                if c == 0:
                    pe.wait_ge(kdec, 2 * b + 2)
                    pe.wait_ge(evacuated, 14 * b + 8)
                if not (is_first(b) and c == 0):
                    pe.wait_ge(s_updated, 2 * (NCH * b + c))

            def gla(b):
                tail = not is_first(b)
                ka_tile(b, 0, (lambda c: pair_out(b - 1, 0, c)) if tail else None)
                ka_tile(b, 1)
                if tail:
                    head_stat(b - 1, 0)
                ka_tile(b, 2)
                if tail:
                    head_stat(b - 1, 1)
                ka_tile(b, 3)

                def second_logits():
                    pe.wait_ge(z_ready, 2 * b + 1)
                    logits(b, 1)

                def stat2():
                    if tail:
                        head_stat(b - 1, 2)

                def first_sums():
                    if tail:
                        pe.wait_ge(head_root, 4 * b)
                    else:
                        pe.wait_ge(z_ready, 2)
                    pe.wait_ge(loga, b + 1)
                    suffix_sums(b, 0)

                def gammas():
                    pe.wait_ge(decay, 2 * b + 2)
                    chunk_sums(b)

                v_tile(b, 0, halfway(lambda: turn_a(b)))
                pe.wait_ge(aT_ready, b + 1)
                logits(b, 0)
                v_tile(b, 1, (lambda c: pair_out(b - 1, 1, c)) if tail else None)
                second_logits()
                v_tile(b, 2, halfway(stat2))
                if tail:
                    head_stat(b - 1, 3)
                v_tile(b, 3)
                gla_tile(b, 8, W_Q)
                gla_tile(b, 9, W_Q + 1, halfway(first_sums))
                pe.wait_ge(decay, 2 * b + 1)
                suffix_sums(b, 1)
                gla_tile(b, 10, W_G, halfway(gammas))
                if not is_last(b):
                    pe.wait_ge(gamma_ready, b + 1)
                    x_stats(b + 1)
                gla_tile(b, 11, W_G + 1, waits=lambda k: increment_waits(b, 0) if k == 7 else None)
                increments(b, 0)
                gla_tile(b, 12, W_G + 2, halfway(lambda: increments(b, 2)),
                         lambda k: increment_waits(b, {3: 2, 7: 4}[k]) if k in (3, 7) else None)
                increments(b, 4)
                gla_tile(b, 13, W_G + 3, halfway(lambda: increments(b, 6)),
                         lambda k: increment_waits(b, 6) if k == 3 else None)

            def conv(b):
                for t in range(16):
                    n = W_CONV + t
                    weights(b, n)
                    if is_first(b) and t < 8:
                        if t < 3:
                            pe.wait_ge(evacuated, 14 * NB - (1, 0, 2)[t])
                        elif t < 5:
                            pe.wait_ge(s_updated, 2 * NCH * NB)
                        elif t < 7:
                            pe.wait_ge(head_step, 3 * (HEADS * NB - 7 + t) + H_SCALED)
                        else:
                            pe.wait_ge(head_root, HEADS * NB)
                    else:
                        wait_conv_read(4 * b - 2 + t // 4, t % 4)
                    big_tile(CONV, b, t, ps[TURN[t % 8]][:], stationary_w(slot_of(n)),
                             (lambda k: last_heads(t, k)) if is_first(b) else None)

            def last_heads(t, k):
                last = NB - 1
                if t == 0:
                    pair_out(last, 0, k)
                    if k == KT - 1:
                        head_stat(last, 0)
                elif t == 1 and k == 3:
                    head_stat(last, 1)
                elif t == 2 and k >= 4:
                    pair_out(last, 1, k - 4)
                elif t == 3 and k == 3:
                    head_stat(last, 2)
                elif t == 3 and k >= 4:
                    pair_out(last, 1, k)
                elif t == 4 and k == 3:
                    head_stat(last, 3)

            def wait_conv_read(j, kind):
                if kind == 0:
                    pe.wait_ge(cc_copied, j + 1)
                elif kind == 1:
                    pe.wait_ge(conv_step, 7 * j + C_U)
                elif kind == 2:
                    pe.wait_ge(silu_ready, j + 1)
                else:
                    pe.wait_ge(conv_step, 7 * j + C_GATED)

            def out_proj(b):
                for m in range(KT):
                    weights(b, W_OUT + m)
                    if is_first(b):
                        wait_conv_read(4 * NB - 2 + m // 4, m % 4)
                    else:
                        pe.wait_ge(h_ready, 8 * (b - 1) + m + 1)
                    big_tile(OUT, b, m, ps[TURN[m]][:], stationary_w(slot_of(W_OUT + m)))

            def wait_out_read(bank):
                pe.wait_ge(h_ready, 8 * (NB - 1) + TURN.index(bank) + 1)

            def gate(b, odd=0):
                for m in range(KT):
                    if is_first(b) and m == 0:
                        pe.wait_ge(w_ready, N_W)
                    if m == 0:
                        pe.wait_ge(p_hi, 2 * (b + 1))
                        pe.wait_ge(p_lo, 2 * (b + 1))
                    if is_first(b) and m < 3:
                        wait_out_read(3 + m)
                    else:
                        pe.wait_ge(gated, 8 * b + m - 2 if m >= 3 else 8 * b - (1, 0, 2)[m])
                    bank = ps[3 + m % 3][:]
                    for k in range(PLE_K):
                        s = slot_of(W_PLE + k)
                        nc.tensor.matmul(bank, WH[:, s, m], PH[:, k], start=(k == 0), stop=False)
                        nc.tensor.matmul(bank, WL[:, s, m], PH[:, k], start=False, stop=False)
                        mm = nc.tensor.matmul(bank, WH[:, s, m], PL[:, k], start=False, stop=(k == PLE_K - 1))
                    mm.then_inc(tile_done[GATE], 1)
                    weights(b, W_GATE + m)
                    if is_first(b) and m < 3:
                        wait_out_read(m)
                    else:
                        pe.wait_ge(gate_ready, 8 * b + m - 2 if m >= 3 else 8 * b - (1, 0, 2)[m])
                    big_tile(GATE, b, 2 * m + 1, ps[m % 3][:], stationary_w(slot_of(W_GATE + m)))
                    if m == 0 and not is_first(b):
                        out_stats(b - 1)

            def out_stats(b):
                pe.wait_ge(out_sum, 8 * (b + 1))
                mean_of(STAT, acc[:]).then_inc(out_mean, 1)

            pe.wait_ge(memsets, 5)
            pe.wait_ge(consts_loaded, 80)
            x_stats(0)
            over_blocks(pe, gla, apart=2)
            over_blocks(pe, conv)
            over_blocks(pe, out_proj)
            over_blocks(pe, gate, pair=True)
            out_stats(NB - 1)

        @block.scalar
        def _(act):
            def split_hi(step, src, phase):
                for k in range(KT):
                    if phase in (GLA, CONV):
                        act.wait_ge(n_ready, 8 * step + k + 1)
                    elif k % 2 == 0:
                        act.wait_ge(raw_loaded[k // 2], 16 * (step + 1))
                    if not (isinstance(step, int) and step == 0):
                        act.wait_ge(x_free, 8 * (step - 1) + k + 1)
                    nc.scalar.activation(XH[:, k], src[:, k], ACT.Copy).then_inc(x_hi, 1)

            def x_squares(s, ks):
                for k in ks:
                    if k % 2 == 0:
                        act.wait_ge(raw_loaded[k // 2], 16 * (s + 1))
                    if k >= 2 or not is_first(s):
                        act.wait_ge(x_sum, 7 * s + (max(1, k - 2) if k >= 2 else 0))
                    nc.scalar.activation(sq[:, k % 2], raw[:, k], ACT.Square).then_inc(x_sq, 1)

            def x_rms(s):
                act.wait_ge(x_mean, s + 1)
                nc.scalar.activation(R[:], ps[SMALL][:], ACT.Sqrt, bias=eps[:], scale=1.0 / D_MODEL).then_inc(
                    x_root, 1)

            def evacuate(b, i, dst, src, func=ACT.Copy, scale=1.0):
                wait_tile(act, GLA, b, i)
                nc.scalar.activation(dst, src, func, scale=scale).then_inc(evacuated, 1)

            def ka_out(b, t):
                if not is_first(b):
                    act.wait_ge(ds_done, NCH * b)
                evacuate(b, t, ka_sb[:, t], ps[MAIN[t % 3]][:, 0:KA])

            def v_out(b, t):
                if not is_first(b):
                    act.wait_ge(ds_done, NCH * b)
                evacuate(b, 4 + t, v_sb[:, t], ps[MAIN[(4 + t) % 3]][:])

            def q_out(b, t):
                if not is_first(b):
                    act.wait_ge(o_done, HEADS * b)
                wait_tile(act, GLA, b, 8 + t)
                for odd in range(2):
                    rows = slice(DK * odd, DK * odd + DK)
                    mm = nc.scalar.activation(
                        q_diag[t][rows, :, odd], ps[MAIN[(8 + t) % 3]][rows, :].rearrange("p (c t) -> p c t", c=NCH),
                        ACT.Copy, scale=DK ** -0.5)
                mm.then_inc(evacuated, 1)

            def g_out(b, h):
                if not is_first(b):
                    act.wait_ge(head_step, 3 * (4 * (b - 1) + h // 2 * 2 + 1) + H_DONE)
                evacuate(b, 10 + h, sg[:, h], ps[MAIN[(10 + h) % 3]][:], ACT.Silu)

            def head_squares(b, h):
                act.wait_ge(o_done, 4 * b + h + 1)
                if h > 0:
                    act.wait_ge(head_mean, 4 * b + h)
                nc.scalar.activation(hsq[:], ps[O_BANK[h % 2]][:], ACT.Square).then_inc(head_sq, 1)

            def head_rms(b, h):
                act.wait_ge(head_mean, 4 * b + h + 1)
                if h > 0:
                    act.wait_ge(head_step, 3 * (4 * b + h - 1) + H_SCALED)
                nc.scalar.activation(rt[:], ps[SMALL][:], ACT.Sqrt, bias=eps[:], scale=1.0 / DV).then_inc(
                    head_root, 1)

            def a_out(b):
                act.wait_ge(aT_done, b + 1)
                if not is_first(b):
                    act.wait_ge(z_done, 2 * b)
                nc.scalar.activation(aT[:], ps[SMALL][0:RANK, :], ACT.Copy).then_inc(aT_ready, 1)

            def log_sigmoid(b):
                act.wait_ge(z_neg, b + 1)
                nc.scalar.activation(tmp[:], tmp[:], ACT.Exp).then_inc(z_exp, 1)

            def log_sigmoid_ln(b):
                act.wait_ge(z_exp, b + 1)
                nc.scalar.activation(tmp[:], tmp[:], ACT.Ln, bias=1.0).then_inc(z_log, 1)

            def decay_out(b, i):
                act.wait_ge(loga, b + 1)
                act.wait_ge(cum_done, 2 * b + i + 1)
                nc.scalar.activation(tmp[:, i], ps[SMALL][:], ACT.Exp).then_inc(decay, 1)

            def gamma_out(b):
                act.wait_ge(gm_done, b + 1)
                if not is_first(b):
                    act.wait_ge(s_updated, 2 * NCH * b)
                nc.scalar.activation(gamma[:].rearrange("p f c -> p (f c)"), ps[SMALL][:, 0:2 * NCH],
                                     ACT.Exp).then_inc(gamma_ready, 1)

            def gla(b):
                tail = not is_first(b)
                nxt = not is_last(b)
                if tail:
                    head_squares(b - 1, 0)
                ka_out(b, 0)
                ka_out(b, 1)
                if tail:
                    head_squares(b - 1, 1)
                    head_rms(b - 1, 0)
                ka_out(b, 2)
                ka_out(b, 3)
                if tail:
                    head_rms(b - 1, 1)
                a_out(b)
                if tail:
                    head_squares(b - 1, 2)
                v_out(b, 0)
                v_out(b, 1)
                if tail:
                    head_squares(b - 1, 3)
                    head_rms(b - 1, 2)
                    head_rms(b - 1, 3)
                if nxt:
                    x_squares(b + 1, (0, 1))
                v_out(b, 2)
                if nxt:
                    x_squares(b + 1, (2, 3))
                log_sigmoid(b)
                v_out(b, 3)
                log_sigmoid_ln(b)
                if nxt:
                    x_squares(b + 1, (4, 5))
                q_out(b, 0)
                decay_out(b, 0)
                if nxt:
                    x_squares(b + 1, (6, 7))
                q_out(b, 1)
                decay_out(b, 1)
                gamma_out(b)
                if nxt:
                    g_out(b, 0)
                    x_rms(b + 1)
                else:
                    g_out(b, 0)
                g_out(b, 1)
                g_out(b, 2)
                split_hi(b + 1, raw, GLA)
                g_out(b, 3)

            def conv(b):
                for j in range(4):
                    if is_first(b) and j == 0:
                        head_squares(NB - 1, 0)
                    if is_first(b) and j == 1:
                        head_rms(NB - 1, 3)
                    wait_tile(act, CONV, b, 4 * j)
                    if not (is_first(b) and j == 0):
                        act.wait_ge(conv_step, 7 * (4 * b + j - 1) + C_U)
                    nc.scalar.activation(ccs[:], ps[TURN[(4 * j) % 8]][:], ACT.Copy).then_inc(cc_copied, 1)
                    if is_first(b) and j == 0:
                        head_squares(NB - 1, 1)
                        head_rms(NB - 1, 0)
                        head_rms(NB - 1, 1)
                        head_squares(NB - 1, 2)
                    wait_tile(act, CONV, b, 4 * j + 2)
                    if not (is_first(b) and j == 0):
                        act.wait_ge(conv_step, 7 * (4 * b + j - 1) + C_DONE)
                    nc.scalar.activation(sgc[:], ps[TURN[(4 * j + 2) % 8]][:], ACT.Silu).then_inc(silu_ready, 1)
                    if is_first(b) and j == 0:
                        head_squares(NB - 1, 3)
                        head_rms(NB - 1, 2)
                split_hi(NB + b + 1, raw, OUT if is_last(b) else CONV)

            def out_proj(b):
                if is_last(b):
                    split_p_hi(0)
                split_hi(2 * NB + b + 1, raw, OUT)

            def split_p_hi(b):
                act.wait_ge(p_loaded, 16 * (b + 1))
                if not is_first(b):
                    wait_tile(act, GATE, b - 1, TILES[GATE] - 2)
                for k in range(PLE_K):
                    nc.scalar.activation(PH[:, k], p_raw[:, k], ACT.Copy).then_inc(p_hi, 1)

            def gate(b, odd=0):
                for m in range(KT):
                    if m == KT - 1 and not is_last(b):
                        split_p_hi(b + 1)
                        split_hi(3 * NB + b + 1, raws[1 - odd], GATE)
                    wait_tile(act, GATE, b, 2 * m + 1)
                    if not (is_first(b) and m < 2):
                        act.wait_ge(gated, 8 * b + m - 1)
                    nc.scalar.activation(gt[:, m % 2], ps[m % 3][:], ACT.Sigmoid,
                                         bias=vec[:, V_BG + m:V_BG + m + 1]).then_inc(gate_ready, 1)
                    if m == 0 and not is_first(b):
                        out_rms(b - 1)
                    act.wait_ge(mixed, 8 * b + m + 1)
                    if not (is_first(b) and m < 2):
                        act.wait_ge(out_sum, 8 * b + m - 1)
                    nc.scalar.activation(osq[:, m % 2], raws[odd][:, m], ACT.Square).then_inc(out_sq, 1)

            def out_rms(b):
                act.wait_ge(out_mean, b + 1)
                nc.scalar.activation(R[:], ps[STAT][:], ACT.Sqrt, bias=eps[:], scale=1.0 / D_MODEL).then_inc(
                    out_root, 1)

            act.wait_ge(memsets, 5)
            nc.scalar.activation(warm[:], eps[:], ACT.Sqrt)
            x_squares(0, range(KT))
            x_rms(0)
            act.wait_ge(consts_loaded, 80)
            split_hi(0, raw, GLA)
            over_blocks(act, gla, apart=2)
            over_blocks(act, conv)
            over_blocks(act, out_proj)
            for c in range(2):
                act.wait_ge(y_stored[c], 16 * 4 * NB)
            over_blocks(act, gate, pair=True)
            out_rms(NB - 1)

        @block.vector
        def _(dve):
            def split_lo(step, src, ks=range(KT)):
                for k in ks:
                    dve.wait_ge(x_hi, 8 * step + k + 1)
                    nc.vector.tensor_tensor(XL[:, k], src[:, k], XH[:, k].bitcast(F32), ALU.subtract).then_inc(
                        x_lo, 1)

            def x_sums(s, ks):
                for k in ks:
                    dve.wait_ge(x_sq, 8 * s + k + 1)
                    if k > 1:
                        dve.wait_ge(x_sum, 7 * s + k - 1)
                    elif s > 0:
                        dve.wait_ge(r_stored, 16 * s)
                    nc.vector.tensor_tensor(R[:], sq[:, 0] if k == 1 else R[:], sq[:, k % 2], ALU.add).then_inc(
                        x_sum, 1)

            def x_recip(s):
                dve.wait_ge(x_root, s + 1)
                nc.vector.reciprocal(R[:], R[:]).then_inc(x_rstd, 1)

            def normalise(step, ks):
                for k in ks:
                    if k % 2 == 0:
                        dve.wait_ge(raw_loaded[k // 2], 16 * (step + 1))
                    nc.vector.scalar_tensor_tensor(out=raw[:, k], in0=raw[:, k],
                                                   scalar=vec[:, V_NORM + k:V_NORM + k + 1], in1=R[:],
                                                   op0=ALU.mult, op1=ALU.mult).then_inc(n_ready, 1)

            def head(b, h):
                n = 4 * b + h
                pair, half = h // 2, h % 2
                tokens = slice(half * TB // 2, (half + 1) * TB // 2)
                flat = y_sb[:, h % 2].rearrange("p (h t) -> p h t", h=2)
                dve.wait_ge(head_root, n + 1)
                nc.vector.reciprocal(rt[:], rt[:]).then_inc(head_step, 1)
                dve.wait_ge(head_step, 3 * n + H_RECIP)
                if not (is_first(b) and h < 2):
                    dve.wait_ge(y_stored[h % 2], 16 * (2 * b + h // 2))
                nc.vector.scalar_tensor_tensor(out=y_sb[:, h % 2], in0=ps[O_BANK[h % 2]][:],
                                               scalar=vec[:, V_GLA:V_GLA + 1], in1=rt[:],
                                               op0=ALU.mult, op1=ALU.mult).then_inc(head_step, 1)
                dve.wait_ge(head_step, 3 * n + H_SCALED)
                dve.wait_ge(evacuated, 14 * b + 12 + 2 * pair)
                nc.vector.tensor_tensor(flat, flat, sg[:, 2 * pair:2 * pair + 2, tokens], ALU.mult).then_inc(
                    head_step, 1)

            def add_bias(b, i):
                dve.wait_ge(z_done, 2 * b + i + 1)
                if i == 0 and not is_first(b):
                    dve.wait_ge(gm_done, b)
                nc.vector.tensor_tensor(L[:, 2 * i:2 * i + 2].rearrange("p t c -> p (t c)"), ps[SMALL][:],
                                        bias2[:], ALU.add).then_inc(z_ready, 1)

            def minus_abs(b):
                dve.wait_ge(z_ready, 2 * b + 2)
                if not is_first(b):
                    dve.wait_ge(kdec, 2 * b)
                z = L[:].rearrange("p t c -> p (t c)")
                nc.vector.scalar_tensor_tensor(out=tmp[:].rearrange("p i c -> p (i c)"), in0=z, scalar=-1.0,
                                               in1=z, op0=ALU.mult, op1=ALU.min).then_inc(z_neg, 1)

            def log_decay(b):
                dve.wait_ge(z_log, b + 1)
                z = L[:].rearrange("p t c -> p (t c)")
                nc.vector.scalar_tensor_tensor(out=z, in0=z, scalar=0.0,
                                               in1=tmp[:].rearrange("p i c -> p (i c)"),
                                               op0=ALU.min, op1=ALU.subtract).then_inc(loga, 1)

            def decay_k(b, i):
                dve.wait_ge(decay, 2 * b + i + 1)
                k = ka_sb[:, 2 * i:2 * i + 2, 0:QK]
                nc.vector.tensor_tensor(k, k, tmp[:, i].rearrange("p (t c) -> p t c", t=2), ALU.mult).then_inc(
                    kdec, 1)

            def state(b, ch):
                dve.wait_ge(ds_done, NCH * b + ch + 1)
                if ch == 0:
                    dve.wait_ge(gamma_ready, b + 1)
                    if not is_first(b):
                        dve.wait_ge(o_done, HEADS * b)
                if not (is_first(b) and ch == 0):
                    dve.wait_ge(s_updated, 2 * (NCH * b + ch))
                for f in range(2):
                    nc.vector.scalar_tensor_tensor(out=hist[:, ch, f], in0=hist[:, (ch - 1) % NCH, f],
                                                   scalar=gamma[:, f, ch:ch + 1],
                                                   in1=ps[DS_BANK[ch % 2]][:, f * DV:f * DV + DV],
                                                   op0=ALU.mult, op1=ALU.add).then_inc(s_updated, 1)

            def gla(b):
                tail = not is_first(b)
                nxt = not is_last(b)
                if tail:
                    head(b - 1, 0)
                    head(b - 1, 1)
                add_bias(b, 0)
                add_bias(b, 1)
                minus_abs(b)
                if tail:
                    head(b - 1, 2)
                    head(b - 1, 3)
                if is_first(b):
                    x_sums(1, range(1, 4))
                log_decay(b)
                if is_first(b):
                    x_sums(1, range(4, 6))
                decay_k(b, 0)
                if is_first(b):
                    x_sums(1, range(6, 8))
                decay_k(b, 1)
                if nxt:
                    x_recip(b + 1)
                    dve.wait_ge(x_rstd, b + 2)
                else:
                    dve.wait_ge(r_loaded, 16)
                normalise(b + 1, range(0, 2))
                state(b, 0)
                state(b, 1)
                normalise(b + 1, range(2, 6))
                state(b, 2)
                state(b, 3)
                normalise(b + 1, range(6, 8))
                for ch in range(4, NCH):
                    state(b, ch)
                split_lo(b + 1, raw)

            def conv(b):
                for j in range(4):
                    n = 4 * b + j
                    if not is_first(b):
                        dve.wait_ge(conv_step, 7 * (n - 4) + C_W2)
                        nc.vector.tensor_copy(u[:, j, 0:2], u[:, j, TB:TB + 2]).then_inc(conv_step, 1)
                    else:
                        nc.vector.memset(u[:, j, 0:2], 0.0).then_inc(conv_step, 1)
                    if is_first(b) and j == 0:
                        head(NB - 1, 0)
                        head(NB - 1, 1)
                    dve.wait_ge(conv_step, 7 * n + C_CARRY)
                    wait_tile(dve, CONV, b, 4 * j + 1)
                    dve.wait_ge(cc_copied, n + 1)
                    nc.vector.tensor_tensor(u[:, j, 2:2 + TB], ccs[:], ps[TURN[(4 * j + 1) % 8]][:],
                                            ALU.mult).then_inc(conv_step, 1)
                    dve.wait_ge(conv_step, 7 * n + C_U)
                    w = V_CW + 3 * j
                    nc.vector.tensor_scalar(cv[:], u[:, j, 0:TB], vec[:, w:w + 1],
                                            vec[:, V_CB + j:V_CB + j + 1], ALU.mult, ALU.add).then_inc(conv_step, 1)
                    for i in (1, 2):
                        dve.wait_ge(conv_step, 7 * n + C_W0 + i - 1)
                        nc.vector.scalar_tensor_tensor(out=cv[:], in0=u[:, j, i:i + TB],
                                                       scalar=vec[:, w + i:w + i + 1], in1=cv[:],
                                                       op0=ALU.mult, op1=ALU.add).then_inc(conv_step, 1)
                    if j == 3:
                        split_lo(NB + b + 1, raw)
                    wait_tile(dve, CONV, b, 4 * j + 3)
                    dve.wait_ge(conv_step, 7 * n + C_W2)
                    nc.vector.tensor_tensor(cv[:], cv[:], ps[TURN[(4 * j + 3) % 8]][:], ALU.mult).then_inc(
                        conv_step, 1)
                    if is_first(b) and j == 0:
                        head(NB - 1, 2)
                        head(NB - 1, 3)
                    dve.wait_ge(conv_step, 7 * n + C_GATED)
                    dve.wait_ge(silu_ready, n + 1)
                    dve.wait_ge(y_stored[j % 2], 16 * (2 * NB + 2 * b + j // 2))
                    nc.vector.tensor_tensor(y_sb[:, j % 2], cv[:], sgc[:], ALU.mult).then_inc(conv_step, 1)
                    if j == 1 and not is_last(b):
                        dve.wait_ge(r_loaded, 16 * (b + 2))
                        normalise(NB + b + 1, range(KT))

            def out_proj(b):
                for m in range(KT):
                    if m == KT - 1:
                        if is_last(b):
                            split_p_lo(0)
                        split_lo(2 * NB + b + 1, raw)
                    wait_tile(dve, OUT, b, m)
                    dve.wait_ge(xt_loaded[m % 4], 16 * (2 * b + m // 4 + 1))
                    nc.vector.tensor_tensor(xt[:, m % 4], xt[:, m % 4], ps[TURN[m]][:], ALU.add).then_inc(
                        h_ready, 1)

            def split_p_lo(b):
                dve.wait_ge(p_hi, 2 * (b + 1))
                for k in range(PLE_K):
                    nc.vector.tensor_tensor(PL[:, k], p_raw[:, k], PH[:, k].bitcast(F32), ALU.subtract).then_inc(
                        p_lo, 1)

            def gate(b, odd=0):
                def add_square(m):
                    dve.wait_ge(out_sq, 8 * b + m + 1)
                    if m == 0:
                        if is_first(b):
                            for c in range(4):
                                dve.wait_ge(h_stored[c], 16 * 2 * NB)
                        else:
                            dve.wait_ge(out_mean, b)
                        nc.vector.tensor_copy(acc[:], osq[:, 0]).then_inc(out_sum, 1)
                    else:
                        dve.wait_ge(out_sum, 8 * b + m)
                        nc.vector.tensor_tensor(acc[:], acc[:], osq[:, m % 2], ALU.add).then_inc(out_sum, 1)

                for m in range(KT):
                    if m == KT - 1 and not is_last(b):
                        split_p_lo(b + 1)
                        split_lo(3 * NB + b + 1, raws[1 - odd])
                    wait_tile(dve, GATE, b, 2 * m)
                    dve.wait_ge(gate_ready, 8 * b + m + 1)
                    if not (is_first(b) and m == 0):
                        dve.wait_ge(mixed, 8 * b + m)
                    nc.vector.tensor_tensor(t_sb[:], gt[:, m % 2], ps[3 + m % 3][:], ALU.mult).then_inc(gated, 1)
                    dve.wait_ge(gated, 8 * b + m + 1)
                    nc.vector.tensor_tensor(raws[odd][:, m], raws[odd][:, m], t_sb[:], ALU.add).then_inc(mixed, 1)
                    if m >= 1:
                        add_square(m - 1)
                    if m == 0 and not is_first(b):
                        final_norm(b - 1, 1 - odd)
                add_square(KT - 1)

            def final_norm(b, odd):
                dve.wait_ge(out_root, b + 1)
                nc.vector.reciprocal(R[:], R[:]).then_inc(out_rstd, 1)
                dve.wait_ge(out_rstd, b + 1)
                for m in range(KT):
                    nc.vector.scalar_tensor_tensor(out=raws[odd][:, m], in0=raws[odd][:, m],
                                                   scalar=vec[:, V_FIN + m:V_FIN + m + 1], in1=R[:],
                                                   op0=ALU.mult, op1=ALU.mult).then_inc(out_norm, 1)

            dve.wait_ge(memsets, 5)
            x_sums(0, range(1, KT))
            x_recip(0)
            dve.wait_ge(consts_loaded, 80)
            dve.wait_ge(x_rstd, 1)
            normalise(0, range(KT))
            dve.wait_ge(x_lo, FIRST_LO)
            split_lo(0, raw, range(FIRST_LO, KT))
            over_blocks(dve, gla, apart=2)
            over_blocks(dve, conv)
            over_blocks(dve, out_proj)
            over_blocks(dve, gate, pair=True)
            final_norm(NB - 1, 1)


def kernel(x, p, norm_w, w_in, w_alpha_up, b_alpha, gla_norm_w, conv_w, conv_b,
           w_out, w_ple, w_ple_gate, b_ple_gate, final_norm_w):
    import numpy as np
    import concourse.bacc as bacc
    from concourse.bass_utils import run_bass_kernel_spmd

    def blocks(a):
        return np.ascontiguousarray(np.asarray(a).reshape(NB, TB, -1, P).transpose(0, 3, 2, 1))

    def tiles(w):
        w = np.asarray(w)
        return np.ascontiguousarray(w.reshape(w.shape[0] // P, P, -1, P).transpose(2, 1, 0, 3)).reshape(
            w.shape[1] // P, P, -1)

    def cols(v):
        return np.asarray(v).reshape(-1, P).T

    w = np.asarray(w_in)[0]
    q, k, v, g, a, cb, cc, cu, gc = np.split(w, np.cumsum([256, 256, 512, 512, 16, 512, 512, 512]), axis=1)
    ka = np.concatenate([k, a], axis=1).reshape(KT, P, KA).transpose(1, 0, 2)
    conv = np.stack([m.reshape(D_MODEL, 4, P) for m in (cc, cu, gc, cb)], axis=2).reshape(D_MODEL, 4 * 512)
    ple = np.asarray(w_ple)[0].reshape(PLE_K, P, D_MODEL)

    r = np.arange(P)
    same = (r[:, None] // CHUNK) == (r[None, :] // CHUNK)
    tau = 16.0
    masks = np.concatenate([(same & (r[:, None] > r[None, :])) / tau,
                            ((r[:, None] // CHUNK) == np.arange(2)[None, :]) / tau, np.eye(P)],
                           axis=1).astype(np.float32)
    cw = np.asarray(conv_w)[0].reshape(3, 4, P).transpose(2, 1, 0).reshape(P, 12)
    vectors = np.concatenate([cols(np.asarray(norm_w)[0]), cols(np.asarray(gla_norm_w)[0]), cw,
                              cols(np.asarray(conv_b)[0]), cols(np.asarray(b_ple_gate)[0]),
                              cols(final_norm_w)], axis=1)
    ba = np.asarray(b_alpha)[0]
    arrays = {
        "xb": blocks(np.asarray(x)[0]), "pb": blocks(np.asarray(p)[0, 0]), "w_ka": ka,
        "w_in": tiles(np.concatenate([v, q, g, conv], axis=1)), "w_out": tiles(np.asarray(w_out)[0]),
        "w_gate": tiles(np.asarray(w_ple_gate)[0]), "w_ple": ple, "w_up": np.asarray(w_alpha_up)[0],
        "b_alpha": np.broadcast_to(np.concatenate([ba, ba]), (P, 2 * QK)), "vectors": vectors, "masks": masks,
    }
    arrays = {f"{n}_dram": np.ascontiguousarray(a) for n, a in arrays.items()}

    nc = bacc.Bacc("TRN2", target_bir_lowering=False, num_devices=1, dynamic_dma_scratch_size=2048)
    args = [nc.dram_tensor(n, a.shape, F32, kind="ExternalInput").ap() for n, a in arrays.items()]
    args.append(nc.dram_tensor("out_dram", (NB, P, KT, TB), F32, kind="ExternalOutput").ap())
    args.append(nc.dram_tensor("y_scratch", (NB, P, KT, TB), F32).ap())
    args.append(nc.dram_tensor("h_scratch", (NB, P, KT, TB), F32).ap())
    args.append(nc.dram_tensor("r_scratch", (NB, P, TB), F32).ap())
    build(nc, *args)
    res = run_bass_kernel_spmd(nc, [arrays], core_ids=[0])
    o = res.results[0]["out_dram"]
    return o.transpose(0, 3, 2, 1).reshape(1, SEQ, D_MODEL)
```

```python
from contextlib import ExitStack

import concourse.bass as bass
from concourse import mybir

P = 128
D_MODEL, SEQ = 1024, 4096
TB = 512
NB = SEQ // TB
KT = D_MODEL // P
HEADS, DK, DV = 4, 64, 128
QK, RANK, CHUNK = HEADS * DK, 16, 64
KA = QK + RANK
TT = TB // P
NCH = TB // CHUNK
PLE_K = 2
EPS = 1e-6
FIRST_LO = 3
V_BY_DVE = 2
HALF_A, HALF_B = slice(0, TB // 2), slice(TB // 2, TB)
SLOTS = 16
BIG = D_MODEL * 4

F32 = mybir.dt.float32
F32R = mybir.dt.float32r
ACT = mybir.ActivationFunctionType
ALU = mybir.AluOpType

GLA, CONV, OUT, GATE = range(4)

V_NORM, V_GLA, V_CW, V_CB, V_BG, V_FIN = 0, 8, 9, 21, 25, 33
N_VEC = 41

W_KA, W_V, W_Q, W_G, W_CONV, W_OUT, W_GATE, W_PLE, N_W = 0, 4, 8, 10, 14, 30, 38, 46, 48
KA_SLOT = 10
RING_ORDER = [10, 11, 12, 0, 1, 2, 3, 4, 5, 6, 7, 8, 9, 13, 14, 15]


def splits(n):
    return n + 1 - V_BY_DVE


def slot_of(n):
    if n < W_CONV:
        return n - W_V
    if n < W_OUT:
        return RING_ORDER[n - W_CONV]
    if n < W_PLE:
        return RING_ORDER[n - W_OUT]
    return RING_ORDER[n - W_PLE]


MAIN = (0, 1, 2)
O_BANK = (3, 4)
DS_BANK = (5, 6)
SMALL = 7
TURN = (0, 1, 2, 5, 6, 3, 4, 7)
STAT = 6

H_RECIP, H_SCALED, H_DONE = 1, 2, 3
C_CARRY, C_U, C_W0, C_W1, C_W2, C_GATED, C_DONE = range(1, 8)
TILES = {GLA: 14, CONV: 16, OUT: 8, GATE: 16}


def build(nc, xb, pb, w_ka, w_in, w_out, w_gate, w_ple, w_up, b_alpha, vectors, masks,
          out, y_scratch, h_scratch, r_scratch):
    with ExitStack() as ctx:
        def sb(name, shape, dt=F32):
            return ctx.enter_context(nc.sbuf_tensor(name, shape, dt))

        def sem(name):
            return ctx.enter_context(nc.semaphore(name))

        def over(name, shape, at, dt=F32):
            return nc.alloc_sbuf_tensor_at(name, shape, dt, offset=at)

        ps = [ctx.enter_context(nc.psum_tensor(f"bank{i}", [P, 512], F32)) for i in range(8)]

        wh_at = (nc.sbuf_base + 31) // 32 * 32
        WH = sb("WH", [P, SLOTS, KT, P], F32R)
        wl_at = wh_at + SLOTS * BIG
        WL = sb("WL", [P, SLOTS, KT, P], F32R)
        XH = sb("XH", [P, KT, TB], F32R)
        XL = sb("XL", [P, KT, TB], F32R)
        raw = sb("raw", [P, KT, TB])
        stage = sb("stage", [P, 2, D_MODEL])
        vec = sb("vec", [P, N_VEC])
        eps = sb("eps", [P, 1])
        warm = sb("warm", [P, 1])
        mask_at = (nc.sbuf_base + 31) // 32 * 32
        mask = sb("mask", [P, P + 2])
        ones = sb("ones", [P, P], F32R)
        y_at = (nc.sbuf_base + 31) // 32 * 32
        y_sb = sb("y_sb", [P, 2, TB])
        L_hi = over("L_hi", [P, 2, 2 * QK], y_at, F32R)
        r_at = (nc.sbuf_base + 31) // 32 * 32
        R = sb("R", [P, TB])
        R_lo = over("R_lo", [P, TB], r_at, F32R)
        suffix = over("suffix", [P, P], mask_at, F32R)
        member = mask[:, P:P + 2]

        KAH = WH[:, KA_SLOT:KA_SLOT + 3].rearrange("p s k c -> p (s k c)")[:, 0:KT * KA].rearrange(
            "p (k c) -> p k c", k=KT)
        KAL = WL[:, KA_SLOT:KA_SLOT + 3].rearrange("p s k c -> p (s k c)")[:, 0:KT * KA].rearrange(
            "p (k c) -> p k c", k=KT)
        tail_at = wh_at + KA_SLOT * BIG + KT * KA * 4
        ident = over("ident", [P, P], tail_at)
        bias2 = over("bias2", [P, 2 * QK], tail_at + P * 4)
        wup = over("wup", [RANK, QK], tail_at + (P + 2 * QK) * 4)
        v_sb = over("v_sb", [P, TT, HEADS * DV], wh_at + 13 * BIG)
        hist = over("hist", [P, NCH, 2, DV], wl_at + 13 * BIG)
        L = over("L", [P, TT, QK], wh_at + 15 * BIG)
        q_diag = [over("q_diag0", [P, NCH, 2, CHUNK], wl_at + 15 * BIG), sb("q_diag1", [P, NCH, 2, CHUNK])]
        raw_odd = over("raw_odd", [P, KT, TB], wh_at)
        raws = (raw, raw_odd)

        ROW = TB * 4
        KA_ROW = TT * KA * 4
        U_ROW = 4 * (2 + TB) * 4
        a_at = (nc.sbuf_base + 31) // 32 * 32
        sb("region_a", [P, (KA_ROW + 5 * ROW) // 4])
        ka_sb = over("ka_sb", [P, TT, KA], a_at)
        sum_hi = over("sum_hi", [P, TB], a_at + KA_ROW, F32R)
        tmp = over("tmp", [P, 2, TB], a_at + KA_ROW + ROW)
        L_lo = over("L_lo", [P, 2, 2 * QK], a_at + KA_ROW + ROW, F32R)
        sq = over("sq", [P, 2, TB], a_at + KA_ROW + 3 * ROW)
        aT = over("aT", [RANK, TB], a_at + KA_ROW + 3 * ROW)
        u = over("u", [P, 4, 2 + TB], a_at)
        ccs = over("ccs", [P, TB], a_at + U_ROW)
        cv = over("cv", [P, TB], a_at + U_ROW + ROW)
        sgc = over("sgc", [P, TB], a_at + U_ROW + 2 * ROW)
        p_raw = over("p_raw", [P, PLE_K, TB], a_at)
        PH = over("PH", [P, PLE_K, TB], a_at + 2 * ROW, F32R)
        PL = over("PL", [P, PLE_K, TB], a_at + 4 * ROW, F32R)
        t_sb = over("t_sb", [P, TB], a_at + 6 * ROW)
        b_at = (nc.sbuf_base + 31) // 32 * 32
        sb("region_b", [P, 6 * TB])
        sg = over("sg", [P, HEADS, TB], b_at)
        hsq = over("hsq", [P, TB], b_at + 4 * ROW)
        hsq_lo = over("hsq_lo", [P, TB], b_at + 4 * ROW, F32R)
        rt = over("rt", [P, TB], b_at + 5 * ROW)
        xt = over("xt", [P, 4, TB], b_at)
        acc = over("acc", [P, TB], b_at)
        acc_lo = over("acc_lo", [P, TB], b_at, F32R)
        acc_hi = over("acc_hi", [P, TB], b_at + ROW, F32R)
        gt = over("gt", [P, 2, TB], b_at + 4 * ROW)
        osq = y_sb
        early_ka = [L[:].rearrange("p t c -> p (t c)"), tmp[:].rearrange("p i c -> p (i c)")]
        early_v3 = over("early_v3", [P, 3, D_MODEL], b_at)
        early_v = [early_v3[:, 0], early_v3[:, 1], early_v3[:, 2], y_sb[:].rearrange("p i c -> p (i c)")]
        gamma = sb("gamma", [P, 2, NCH])

        consts_loaded = sem("consts_loaded")
        memsets = sem("memsets")
        stage_loaded = [sem(f"stage_loaded{i}") for i in range(2)]
        early_loaded = [sem(f"early_loaded{i}") for i in range(6)]
        w_hi = sem("w_hi")
        v_hi = sem("v_hi")
        v_lo = sem("v_lo")
        w_ready = sem("w_ready")
        raw_loaded = [sem(f"raw_loaded{i}") for i in range(4)]
        first_rstd, first_n, first_hi, first_lo = (sem(f"first_{i}") for i in ("rstd", "n", "hi", "lo"))
        n_ready = sem("n_ready")
        x_hi = sem("x_hi")
        x_lo = sem("x_lo")
        x_free = sem("x_free")
        tile_done = [sem(f"tile_done_{n}") for n in ("gla", "conv", "out", "gate")]
        x_sq = sem("x_sq")
        x_sum = sem("x_sum")
        x_sum_hi = sem("x_sum_hi")
        x_split = sem("x_split")
        x_mean = sem("x_mean")
        x_root = sem("x_root")
        x_rstd = sem("x_rstd")
        r_stored = sem("r_stored")
        r_loaded = sem("r_loaded")
        evacuated = sem("evacuated")
        aT_done = sem("aT_done")
        aT_ready = sem("aT_ready")
        z_done = sem("z_done")
        z_ready = sem("z_ready")
        z_neg = sem("z_neg")
        z_exp = sem("z_exp")
        z_log = sem("z_log")
        loga = sem("loga")
        loga_hi = sem("loga_hi")
        loga_split = sem("loga_split")
        suffix_ready = sem("suffix_ready")
        cum_done = sem("cum_done")
        decay = sem("decay")
        kdec = sem("kdec")
        gm_done = sem("gm_done")
        gamma_ready = sem("gamma_ready")
        ds_done = sem("ds_done")
        s_updated = sem("s_updated")
        o_done = sem("o_done")
        head_sq = sem("head_sq")
        head_split = sem("head_split")
        head_mean = sem("head_mean")
        head_root = sem("head_root")
        head_step = sem("head_step")
        y_stored = [sem(f"y_stored{i}") for i in range(2)]
        cc_copied = sem("cc_copied")
        silu_ready = sem("silu_ready")
        conv_step = sem("conv_step")
        xt_loaded = [sem(f"xt_loaded{i}") for i in range(4)]
        h_ready = sem("h_ready")
        h_stored = [sem(f"h_stored{i}") for i in range(4)]
        p_loaded = sem("p_loaded")
        p_hi = sem("p_hi")
        p_lo = sem("p_lo")
        gate_ready = sem("gate_ready")
        gated = sem("gated")
        mixed = sem("mixed")
        out_sq = sem("out_sq")
        out_sum = sem("out_sum")
        out_sum_hi = sem("out_sum_hi")
        out_split = sem("out_split")
        out_mean = sem("out_mean")
        out_root = sem("out_root")
        out_rstd = sem("out_rstd")
        out_norm = sem("out_norm")
        out_stored = [sem(f"out_stored{i}") for i in range(4)]

        def wait_tile(eng, phase, b, i):
            if i == TILES[phase] - 1:
                eng.wait_ge(x_free, 8 * (8 * phase + b + 1))
            else:
                eng.wait_ge(tile_done[phase], (TILES[phase] - 1) * b + i + 1)

        def over_blocks(eng, body, pair=False, apart=1):
            for b in range(apart):
                body(b)
            if pair:
                with eng.Fori(1, NB - 2, 2) as b:
                    body(b, 1)
                    body(b + 1, 0)
            else:
                with eng.Fori(apart, NB - 1) as b:
                    body(b)
            body(NB - 1, 1) if pair else body(NB - 1)

        def is_first(b):
            return isinstance(b, int) and b == 0

        def is_last(b):
            return isinstance(b, int) and b == NB - 1

        block = ctx.enter_context(nc.Block())

        @block.sync
        def _(sp):
            def load_raw(dst, src, step):
                for c in range(4):
                    sp.dma_start(dst[:, 2 * c:2 * c + 2], src[:, 2 * c:2 * c + 2]).then_inc(raw_loaded[c], 16)

            def store_y(n, b, k):
                sp.dma_start(y_scratch[b, :, k], y_sb[:, k % 2]).then_inc(y_stored[k % 2], 16)

            def store_r(b):
                sp.wait_ge(x_rstd, b + 1)
                sp.dma_start(r_scratch[b], R[:]).then_inc(r_stored, 16)

            def store_heads(b):
                for h in range(HEADS):
                    sp.wait_ge(head_step, 3 * (4 * b + h) + H_DONE)
                    tokens = slice(h % 2 * TB // 2, (h % 2 + 1) * TB // 2)
                    sp.dma_start(y_scratch[b, :, h // 2 * 2:h // 2 * 2 + 2, tokens],
                                 y_sb[:, h % 2].rearrange("p (h t) -> p h t", h=2)).then_inc(y_stored[h % 2], 16)

            def gla(b):
                sp.wait_ge(x_lo, 8 * (b + 1))
                load_raw(raw, xb[0] if is_last(b) else xb[b + 1], b + 1)
                if not is_first(b):
                    store_heads(b - 1)
                if is_last(b):
                    sp.wait_ge(r_stored, 16 * NB)
                    sp.wait_ge(n_ready, 8 * NB)
                    sp.dma_start(R[:], r_scratch[0]).then_inc(r_loaded, 16)
                else:
                    store_r(b + 1)

            def conv(b):
                sp.wait_ge(x_lo, 8 * (NB + b + 1))
                if is_last(b):
                    sp.wait_ge(y_stored[0], 16 * (2 * NB + 2 * (NB - 1)))
                    sp.wait_ge(y_stored[1], 16 * (2 * NB + 2 * (NB - 1)))
                    load_raw(raw, y_scratch[0], 2 * NB)
                else:
                    load_raw(raw, xb[b + 1], NB + b + 1)
                    sp.wait_ge(n_ready, 8 * (NB + b + 1))
                    sp.dma_start(R[:], r_scratch[b + 1]).then_inc(r_loaded, 16)
                if is_first(b):
                    store_heads(NB - 1)
                for j in range(4):
                    sp.wait_ge(conv_step, 7 * (4 * b + j) + C_DONE)
                    store_y(4 * NB + 4 * b + j, b, 4 + j)

            def load_xt(b, m):
                sp.dma_start(xt[:, m % 4], xb[b, :, m]).then_inc(xt_loaded[m % 4], 16)

            def out_proj(b):
                sp.wait_ge(x_lo, 8 * (2 * NB + b + 1))
                if is_last(b):
                    for c in range(4):
                        sp.wait_ge(h_stored[c], 16 * 2 * (NB - 1))
                    load_raw(raw, h_scratch[0], 3 * NB)
                    sp.dma_start(p_raw[:], pb[0]).then_inc(p_loaded, 16)
                else:
                    for c in range(2):
                        sp.wait_ge(y_stored[c], 16 * 4 * NB)
                    load_raw(raw, y_scratch[b + 1], 2 * NB + b + 1)
                for m in range(KT):
                    sp.wait_ge(h_ready, 8 * b + m + 1)
                    sp.dma_start(h_scratch[b, :, m], xt[:, m % 4]).then_inc(h_stored[m % 4], 16)
                    if is_last(b) and m + 2 >= KT:
                        continue
                    if not is_first(b) or m >= 2:
                        sp.wait_ge(h_stored[(m + 2) % 4], 16 * (2 * b + (m + 2) // 4))
                    if m + 2 < KT:
                        load_xt(b, m + 2)
                    else:
                        load_xt(b + 1, m + 2 - KT)

            def store_out(b, odd):
                for c in range(4):
                    sp.wait_ge(out_norm, 8 * b + 2 * c + 2)
                    sp.dma_start(out[b, :, 2 * c:2 * c + 2], raws[odd][:, 2 * c:2 * c + 2]).then_inc(
                        out_stored[c], 16)

            def gate(b, odd=0):
                if not is_last(b):
                    sp.wait_ge(p_lo, 2 * (b + 1))
                    sp.dma_start(p_raw[:], pb[b + 1]).then_inc(p_loaded, 16)
                if is_first(b):
                    sp.wait_ge(x_free, 8 * 3 * NB)
                    for c in range(4):
                        sp.wait_ge(h_stored[c], 16 * 2 * NB)
                else:
                    store_out(b - 1, 1 - odd)
                if not is_last(b):
                    if not is_first(b):
                        for c in range(4):
                            sp.wait_ge(out_stored[c], 16 * b)
                    load_raw(raws[1 - odd], h_scratch[b + 1], 3 * NB + b + 1)

            load_raw(raw, xb[0], 0)
            for i in range(2):
                sp.dma_start(early_ka[i][:, 0:2 * KA], w_ka[:, 4 + 2 * i:6 + 2 * i].rearrange("p k c -> p (k c)")).then_inc(
                    early_loaded[i], 16)
            sp.dma_start(vec[:], vectors).then_inc(consts_loaded, 16)
            sp.dma_start(mask[:], masks[:, 0:P + 2]).then_inc(consts_loaded, 16)
            sp.dma_start(ident[:], masks[:, P + 2:]).then_inc(consts_loaded, 16)
            sp.dma_start(bias2[:], b_alpha).then_inc(consts_loaded, 16)
            sp.dma_start(wup[:], w_up).then_inc(consts_loaded, 16)
            for i in range(4):
                sp.dma_start(early_v[i], w_in[i]).then_inc(early_loaded[2 + i], 16)
            store_r(0)
            over_blocks(sp, gla, apart=2)
            over_blocks(sp, conv)
            load_xt(0, 0)
            load_xt(0, 1)
            over_blocks(sp, out_proj)
            over_blocks(sp, gate, pair=True)
            store_out(NB - 1, 1)
            for c in range(4):
                sp.wait_ge(out_stored[c], 16 * NB)

        @block.gpsimd
        def _(pool):
            pool.memset(ones[:].bitcast(F32), 1.0).then_inc(memsets, 1)
            pool.memset(eps[:], EPS).then_inc(memsets, 1)
            pool.memset(hist[:, NCH - 1], 0.0).then_inc(memsets, 1)
            for pair in range(2):
                pool.memset(q_diag[pair][:], 0.0).then_inc(memsets, 1)

            def source(n):
                if n < W_V:
                    return w_ka[:, 2 * n:2 * n + 2].rearrange("p k c -> p (k c)")
                if n < W_OUT:
                    return w_in[n - W_V]
                if n < W_GATE:
                    return w_out[n - W_OUT]
                if n < W_PLE:
                    return w_gate[n - W_GATE]
                return w_ple[n - W_PLE]

            def load(n):
                if n >= W_Q + 2:
                    pool.wait_ge(w_ready, splits(n - 2))
                src = source(n)
                pool.dma_start(stage[:, n % 2, 0:src.shape[1]], src).then_inc(stage_loaded[n % 2], 16)

            def wait_slot_free(n):
                if n < W_CONV:
                    return
                if n < W_OUT:
                    s = slot_of(n)
                    if s >= 13:
                        pool.wait_ge(o_done, HEADS * NB)
                    elif s == KA_SLOT + 2:
                        pool.wait_ge(z_ready, 2 * NB)
                    elif s >= KA_SLOT:
                        wait_tile(pool, GLA, NB - 1, 3)
                    elif s < 4:
                        wait_tile(pool, GLA, NB - 1, 7)
                    else:
                        wait_tile(pool, GLA, NB - 1, 4 + s)
                elif n < W_PLE:
                    wait_tile(pool, CONV, NB - 1, n - W_OUT)
                else:
                    wait_tile(pool, OUT, NB - 1, n - W_PLE)

            def x_sums(s):
                for k in range(1, KT):
                    pool.wait_ge(x_sq, 8 * s + k + 1)
                    if k == 1:
                        pool.wait_ge(n_ready, 8 * s)
                        pool.wait_ge(r_stored, 16 * s)
                    else:
                        pool.wait_ge(x_sum, 7 * s + k - 1)
                    pool.tensor_tensor(R[:], sq[:, 0] if k == 1 else R[:], sq[:, k % 2], ALU.add).then_inc(
                        x_sum, 1)
                pool.wait_ge(x_sum_hi, s)
                pool.tensor_tensor(R_lo[:], R[:], sum_hi[:].bitcast(F32), ALU.subtract).then_inc(x_split, 1)

            def lo_of_block_0(half, hi_done, lo_done):
                for k in range(FIRST_LO):
                    pool.wait_ge(hi_done, k + 1)
                    pool.tensor_tensor(XL[:, k, half], raw[:, k, half], XH[:, k, half].bitcast(F32),
                                       ALU.subtract).then_inc(lo_done, 1)

            load(0)
            load(1)
            for n in range(N_W):
                if n == W_CONV:
                    x_sums(2)
                    with pool.Fori(3, NB) as s:
                        x_sums(s)
                if W_Q < n < N_W - 1:
                    load(n + 1)
                if n == W_V:
                    lo_of_block_0(HALF_A, first_hi, first_lo)
                    pool.wait_ge(w_ready, 2)
                    load(W_Q)
                    load(W_Q + 1)
                if n == W_V + 1:
                    lo_of_block_0(HALF_B, x_hi, x_lo)
                if W_Q - V_BY_DVE <= n < W_Q:
                    continue
                if 2 <= n < W_Q:
                    source_tile = early_ka[n - 2] if n < W_V else early_v[n - W_V]
                    pool.wait_ge(early_loaded[n - 2], 16)
                else:
                    source_tile = stage[:, n % 2]
                    pool.wait_ge(stage_loaded[n % 2], 16 * (n // 2 + 1 if n < 2 else n // 2 - 2))
                wait_slot_free(n)
                if n < W_V:
                    hi, lo = KAH[:, 2 * n:2 * n + 2], KAL[:, 2 * n:2 * n + 2]
                    src = source_tile[:, 0:2 * KA].rearrange("p (k c) -> p k c", k=2)
                else:
                    hi, lo = WH[:, slot_of(n)], WL[:, slot_of(n)]
                    src = source_tile.rearrange("p (k c) -> p k c", k=KT)
                if W_V < n < W_Q:
                    pool.wait_ge(v_hi, n - W_V)
                else:
                    pool.tensor_scalar(hi, src, 1.0, 0.0, ALU.mult, ALU.add).then_inc(w_hi, 1)
                    pool.wait_ge(w_hi, n + 1 if n <= W_V else n - 2)
                pool.tensor_tensor(lo, src, hi.bitcast(F32), ALU.subtract).then_inc(w_ready, 1)

        @block.tensor
        def _(pe):
            def big_tile(phase, b, i, acc_ap, products, after=None, waits=None):
                step = 8 * phase + b
                last = i == TILES[phase] - 1
                ahead = phase == GLA and is_first(b) and i == 0
                first = i == (1 if phase == GATE else 2 if phase == GLA and is_first(b) else 0)
                for k in range(KT):
                    hh, lh, hl = products(k)
                    if ahead:
                        pe.wait_ge(first_hi, k + 1)
                    elif first:
                        pe.wait_ge(x_hi, 8 * step + k + 1)
                    nc.tensor.matmul(acc_ap, hh[0], hh[1], start=(k == 0), stop=False)
                    nc.tensor.matmul(acc_ap, lh[0], lh[1], start=False, stop=False)
                    if ahead:
                        pe.wait_ge(first_lo, k + 1)
                    elif first:
                        pe.wait_ge(x_lo, 8 * step + k + 1)
                    if waits is not None:
                        waits(k)
                    mm = nc.tensor.matmul(acc_ap, hl[0], hl[1], start=False, stop=(k == KT - 1))
                    if last:
                        mm.then_inc(x_free, 1)
                    elif k == KT - 1:
                        mm.then_inc(tile_done[phase], 1)
                    if after is not None:
                        after(k)

            def halfway(small):
                return lambda k: small() if k == 3 else None

            def stationary_w(slot):
                return lambda k: ((WH[:, slot, k], XH[:, k]), (WL[:, slot, k], XH[:, k]),
                                  (WH[:, slot, k], XL[:, k]))

            def weights(b, n):
                if is_first(b):
                    pe.wait_ge(w_ready, splits(n))

            def mean_of(bank, src):
                return nc.tensor.matmul(ps[bank][:], ones[:].bitcast(F32), src, start=True, stop=True)

            def mean_of_split(bank, hi, lo):
                nc.tensor.matmul(ps[bank][:], ones[:], hi, start=True, stop=False)
                return nc.tensor.matmul(ps[bank][:], ones[:], lo, start=False, stop=True)

            def x_stats(s):
                if is_first(s):
                    pe.wait_ge(x_sum, 7)
                    mean_of(SMALL, R[:]).then_inc(x_mean, 1)
                else:
                    pe.wait_ge(x_split, s)
                    mean_of_split(SMALL, sum_hi[:], R_lo[:]).then_inc(x_mean, 1)

            def main_bank(b, i):
                if i >= 3:
                    pe.wait_ge(evacuated, 14 * b + i - 2)
                elif not is_first(b):
                    pe.wait_ge(evacuated, 14 * b - (1, 0, 2)[i] if i != 2 else 14 * b - 2)
                return ps[MAIN[i % 3]]

            def ka_tile(b, t, after=None):
                if is_first(b):
                    pe.wait_ge(w_ready, W_V)
                tok = slice(t * P, t * P + P)
                big_tile(GLA, b, t, main_bank(b, t)[:, 0:KA],
                         lambda k: ((XH[:, k, tok], KAH[:, k]), (XH[:, k, tok], KAL[:, k]),
                                    (XL[:, k, tok], KAH[:, k])), after)

            def v_tile(b, t, after=None):
                if is_first(b):
                    pe.wait_ge(w_ready, W_Q - V_BY_DVE)
                    pe.wait_ge(v_lo, V_BY_DVE)
                tok = slice(t * P, t * P + P)
                bank = main_bank(b, 4 + t)[:, :].rearrange("p (s c) -> p s c", s=4)
                big_tile(GLA, b, 4 + t, bank,
                         lambda k: ((XH[:, k, tok], WH[:, 0:4, k]), (XH[:, k, tok], WL[:, 0:4, k]),
                                    (XL[:, k, tok], WH[:, 0:4, k])), after)

            def gla_tile(b, i, n, after=None, waits=None):
                weights(b, n)
                big_tile(GLA, b, i, main_bank(b, i)[:], stationary_w(slot_of(n)), after, waits)

            def pair_out(b, pair, c):
                half = c // (NCH // 2)
                if c == 0 and pair == 0:
                    pe.wait_ge(s_updated, 2 * NCH * (b + 1))
                elif pair == 1 and c % (NCH // 2) == 0:
                    pe.wait_ge(head_step, 3 * (4 * b + half) + H_SCALED)
                bank = ps[O_BANK[half]][:].rearrange("p (h c t) -> p h c t", h=2, c=NCH // 2)
                mm = nc.tensor.matmul(bank[:, :, c % (NCH // 2)], hist[:, c, pair], q_diag[pair][:, c],
                                      start=True, stop=True)
                if c % (NCH // 2) == NCH // 2 - 1:
                    mm.then_inc(o_done, 1)

            def head_stat(b, h):
                if h == 0 and is_last(b):
                    pe.wait_ge(gamma_ready, b + 1)
                elif h == 0:
                    pe.wait_ge(x_root, b + 2)
                elif h == 2 and is_last(b):
                    pe.wait_ge(head_root, 4 * b + h)
                elif h == 2:
                    pe.wait_ge(z_ready, 2 * b + 4)
                else:
                    pe.wait_ge(head_root, 4 * b + h)
                pe.wait_ge(head_split, 4 * b + h + 1)
                mean_of_split(SMALL, sum_hi[:], hsq_lo[:]).then_inc(head_mean, 1)

            def turn_a(b):
                pe.wait_ge(evacuated, 14 * b + 4)
                if is_first(b):
                    pe.wait_ge(x_root, 1)
                else:
                    pe.wait_ge(head_root, 4 * (b - 1) + 2)
                for t in range(TT):
                    mm = nc.tensor.transpose(ps[SMALL][0:RANK, t * P:t * P + P], ka_sb[:, t, QK:KA], ident[:])
                mm.then_inc(aT_done, 1)

            def logits(b, i):
                for t in range(2 * i, 2 * i + 2):
                    mm = nc.tensor.matmul(ps[SMALL][:, (t % 2) * QK:(t % 2) * QK + QK],
                                          aT[:, t * P:t * P + P], wup[:], start=True, stop=True)
                mm.then_inc(z_done, 1)

            def suffix_sums(b, i):
                pe.wait_ge(loga_split, 2 * b + i + 1)
                nc.tensor.matmul(ps[SMALL][:], suffix[:], L_hi[:, i], start=True, stop=False)
                nc.tensor.matmul(ps[SMALL][:], suffix[:], L_lo[:, i], start=False, stop=True).then_inc(cum_done, 1)

            def chunk_sums(b):
                for f in range(2):
                    for t in range(TT):
                        mm = nc.tensor.matmul(ps[SMALL][:, f * NCH + 2 * t:f * NCH + 2 * t + 2],
                                              L[:, t, f * P:f * P + P], member, start=True, stop=True)
                mm.then_inc(gm_done, 1)

            def increments(b, c):
                for h in range(HEADS):
                    for ch in (c, c + 1):
                        rows = slice(CHUNK * (ch % 2), CHUNK * (ch % 2) + CHUNK)
                        mm = nc.tensor.matmul(
                            ps[DS_BANK[ch % 2]][DK * (h % 2):DK * (h % 2) + DK, (h // 2) * DV:(h // 2) * DV + DV],
                            ka_sb[rows, ch // 2, h * DK:h * DK + DK],
                            v_sb[rows, ch // 2, h * DV:h * DV + DV], start=True, stop=True)
                        if h == HEADS - 1:
                            mm.then_inc(ds_done, 1)

            def increment_waits(b, c):
                if c == 0:
                    pe.wait_ge(kdec, 2 * b + 2)
                    pe.wait_ge(evacuated, 14 * b + 8)
                if not (is_first(b) and c == 0):
                    pe.wait_ge(s_updated, 2 * (NCH * b + c))

            def gla(b):
                tail = not is_first(b)
                ka_tile(b, 0, (lambda c: pair_out(b - 1, 0, c)) if tail else None)
                ka_tile(b, 1)
                if tail:
                    head_stat(b - 1, 0)
                ka_tile(b, 2)
                ka_tile(b, 3, halfway(lambda: head_stat(b - 1, 1)) if tail else None)

                def second_logits():
                    pe.wait_ge(z_ready, 2 * b + 1)
                    logits(b, 1)

                def stat2():
                    if tail:
                        head_stat(b - 1, 2)

                def first_sums():
                    if tail:
                        pe.wait_ge(head_root, 4 * b)
                    else:
                        pe.wait_ge(z_ready, 2)
                    suffix_sums(b, 0)

                def gammas():
                    pe.wait_ge(decay, 2 * b + 2)
                    chunk_sums(b)

                v_tile(b, 0, halfway(lambda: turn_a(b)))
                pe.wait_ge(aT_ready, b + 1)
                logits(b, 0)
                v_tile(b, 1, (lambda c: pair_out(b - 1, 1, c)) if tail else None)
                second_logits()
                v_tile(b, 2, halfway(stat2))
                if tail:
                    head_stat(b - 1, 3)
                v_tile(b, 3)
                gla_tile(b, 8, W_Q)
                gla_tile(b, 9, W_Q + 1, halfway(first_sums))
                pe.wait_ge(decay, 2 * b + 1)
                suffix_sums(b, 1)
                gla_tile(b, 10, W_G, halfway(gammas))
                if not is_last(b):
                    pe.wait_ge(gamma_ready, b + 1)
                    x_stats(b + 1)
                gla_tile(b, 11, W_G + 1, waits=lambda k: increment_waits(b, 0) if k == 7 else None)
                increments(b, 0)
                gla_tile(b, 12, W_G + 2, halfway(lambda: increments(b, 2)),
                         lambda k: increment_waits(b, {3: 2, 7: 4}[k]) if k in (3, 7) else None)
                increments(b, 4)
                gla_tile(b, 13, W_G + 3, halfway(lambda: increments(b, 6)),
                         lambda k: increment_waits(b, 6) if k == 3 else None)

            def conv(b):
                for t in range(16):
                    n = W_CONV + t
                    weights(b, n)
                    if is_first(b) and t < 8:
                        if t < 3:
                            pe.wait_ge(evacuated, 14 * NB - (1, 0, 2)[t])
                        elif t < 5:
                            pe.wait_ge(s_updated, 2 * NCH * NB)
                        elif t < 7:
                            pe.wait_ge(head_step, 3 * (HEADS * NB - 7 + t) + H_SCALED)
                        else:
                            pe.wait_ge(head_root, HEADS * NB)
                    else:
                        wait_conv_read(4 * b - 2 + t // 4, t % 4)
                    big_tile(CONV, b, t, ps[TURN[t % 8]][:], stationary_w(slot_of(n)),
                             (lambda k: last_heads(t, k)) if is_first(b) else None)

            def last_heads(t, k):
                last = NB - 1
                if t == 0:
                    pair_out(last, 0, k)
                    if k == KT - 1:
                        head_stat(last, 0)
                elif t == 1 and k == KT - 1:
                    head_stat(last, 1)
                elif t == 2 and k >= 4:
                    pair_out(last, 1, k - 4)
                elif t == 3 and k == 3:
                    head_stat(last, 2)
                elif t == 3 and k >= 4:
                    pair_out(last, 1, k)
                elif t == 4 and k == 5:
                    head_stat(last, 3)

            def wait_conv_read(j, kind):
                if kind == 0:
                    pe.wait_ge(cc_copied, j + 1)
                elif kind == 1:
                    pe.wait_ge(conv_step, 7 * j + C_U)
                elif kind == 2:
                    pe.wait_ge(silu_ready, j + 1)
                else:
                    pe.wait_ge(conv_step, 7 * j + C_GATED)

            def out_proj(b):
                for m in range(KT):
                    weights(b, W_OUT + m)
                    if is_first(b):
                        wait_conv_read(4 * NB - 2 + m // 4, m % 4)
                    else:
                        pe.wait_ge(h_ready, 8 * (b - 1) + m + 1)
                    big_tile(OUT, b, m, ps[TURN[m]][:], stationary_w(slot_of(W_OUT + m)))

            def wait_out_read(bank):
                pe.wait_ge(h_ready, 8 * (NB - 1) + TURN.index(bank) + 1)

            def gate(b, odd=0):
                for m in range(KT):
                    if is_first(b) and m == 0:
                        pe.wait_ge(w_ready, splits(N_W - 1))
                    if m == 0:
                        pe.wait_ge(p_hi, 2 * (b + 1))
                        pe.wait_ge(p_lo, 2 * (b + 1))
                    if is_first(b) and m < 3:
                        wait_out_read(3 + m)
                    else:
                        pe.wait_ge(gated, 8 * b + m - 2 if m >= 3 else 8 * b - (1, 0, 2)[m])
                    bank = ps[3 + m % 3][:]
                    for k in range(PLE_K):
                        s = slot_of(W_PLE + k)
                        nc.tensor.matmul(bank, WH[:, s, m], PH[:, k], start=(k == 0), stop=False)
                        nc.tensor.matmul(bank, WL[:, s, m], PH[:, k], start=False, stop=False)
                        mm = nc.tensor.matmul(bank, WH[:, s, m], PL[:, k], start=False, stop=(k == PLE_K - 1))
                    mm.then_inc(tile_done[GATE], 1)
                    if m == 1 and not is_first(b):
                        out_stats(b - 1)
                    weights(b, W_GATE + m)
                    if is_first(b) and m < 3:
                        wait_out_read(m)
                    else:
                        pe.wait_ge(gate_ready, 8 * b + m - 2 if m >= 3 else 8 * b - (1, 0, 2)[m])
                    big_tile(GATE, b, 2 * m + 1, ps[m % 3][:], stationary_w(slot_of(W_GATE + m)))

            def out_stats(b):
                if is_last(b):
                    pe.wait_ge(out_sum, 8 * b + KT - 1)
                    nc.tensor.matmul(ps[STAT][:], ones[:].bitcast(F32), acc[:], start=True, stop=False)
                    pe.wait_ge(out_sq, 8 * b + KT)
                    nc.tensor.matmul(ps[STAT][:], ones[:].bitcast(F32), osq[:, (KT - 1) % 2], start=False,
                                     stop=True).then_inc(out_mean, 1)
                else:
                    pe.wait_ge(out_split, b + 1)
                    mean_of_split(STAT, acc_hi[:], acc_lo[:]).then_inc(out_mean, 1)

            pe.wait_ge(memsets, 5)
            pe.wait_ge(consts_loaded, 80)
            x_stats(0)
            pe.wait_ge(suffix_ready, 1)
            over_blocks(pe, gla, apart=2)
            over_blocks(pe, conv)
            over_blocks(pe, out_proj)
            over_blocks(pe, gate, pair=True)
            out_stats(NB - 1)

        @block.scalar
        def _(act):
            def split_hi(step, src, phase):
                for k in range(KT):
                    if phase in (GLA, CONV):
                        act.wait_ge(n_ready, 8 * step + k + 1)
                    elif k % 2 == 0:
                        act.wait_ge(raw_loaded[k // 2], 16 * (step + 1))
                    if not (isinstance(step, int) and step == 0):
                        act.wait_ge(x_free, 8 * (step - 1) + k + 1)
                    nc.scalar.activation(XH[:, k], src[:, k], ACT.Copy).then_inc(x_hi, 1)

            def x_squares(s, ks):
                for k in ks:
                    if k % 2 == 0:
                        act.wait_ge(raw_loaded[k // 2], 16 * (s + 1))
                    if k >= 2 or not is_first(s):
                        act.wait_ge(x_sum, 7 * s + (max(1, k - 2) if k >= 2 else 0))
                    if k == 0 and not is_first(s):
                        act.wait_ge(z_done, 2 * s)
                    nc.scalar.activation(sq[:, k % 2], raw[:, k], ACT.Square).then_inc(x_sq, 1)

            def x_sum_out(s):
                act.wait_ge(x_sum, 7 * (s + 1))
                nc.scalar.activation(sum_hi[:], R[:], ACT.Copy).then_inc(x_sum_hi, 1)

            def x_rms(s):
                act.wait_ge(x_mean, s + 1)
                nc.scalar.activation(R[:], ps[SMALL][:], ACT.Sqrt, bias=eps[:], scale=1.0 / D_MODEL).then_inc(
                    x_root, 1)

            def evacuate(b, i, dst, src, func=ACT.Copy, scale=1.0):
                wait_tile(act, GLA, b, i)
                nc.scalar.activation(dst, src, func, scale=scale).then_inc(evacuated, 1)

            def ka_out(b, t):
                if not is_first(b):
                    act.wait_ge(ds_done, NCH * b)
                evacuate(b, t, ka_sb[:, t], ps[MAIN[t % 3]][:, 0:KA])

            def v_out(b, t):
                if not is_first(b):
                    act.wait_ge(ds_done, NCH * b)
                evacuate(b, 4 + t, v_sb[:, t], ps[MAIN[(4 + t) % 3]][:])

            def q_out(b, t):
                if not is_first(b):
                    act.wait_ge(o_done, HEADS * b)
                wait_tile(act, GLA, b, 8 + t)
                for odd in range(2):
                    rows = slice(DK * odd, DK * odd + DK)
                    mm = nc.scalar.activation(
                        q_diag[t][rows, :, odd], ps[MAIN[(8 + t) % 3]][rows, :].rearrange("p (c t) -> p c t", c=NCH),
                        ACT.Copy, scale=DK ** -0.5)
                mm.then_inc(evacuated, 1)

            def g_out(b, h):
                if not is_first(b):
                    act.wait_ge(head_step, 3 * (4 * (b - 1) + h // 2 * 2 + 1) + H_DONE)
                evacuate(b, 10 + h, sg[:, h], ps[MAIN[(10 + h) % 3]][:], ACT.Silu)

            def head_squares(b, h):
                act.wait_ge(o_done, 4 * b + h + 1)
                if h > 0:
                    act.wait_ge(head_mean, 4 * b + h)
                nc.scalar.activation(hsq[:], ps[O_BANK[h % 2]][:], ACT.Square)
                nc.scalar.activation(sum_hi[:], ps[O_BANK[h % 2]][:], ACT.Square).then_inc(head_sq, 1)

            def head_rms(b, h):
                act.wait_ge(head_mean, 4 * b + h + 1)
                if h > 0:
                    act.wait_ge(head_step, 3 * (4 * b + h - 1) + H_SCALED)
                nc.scalar.activation(rt[:], ps[SMALL][:], ACT.Sqrt, bias=eps[:], scale=1.0 / DV).then_inc(
                    head_root, 1)

            def a_out(b):
                act.wait_ge(aT_done, b + 1)
                if not is_first(b):
                    act.wait_ge(z_done, 2 * b)
                nc.scalar.activation(aT[:], ps[SMALL][0:RANK, :], ACT.Copy).then_inc(aT_ready, 1)

            def log_sigmoid(b):
                act.wait_ge(z_neg, b + 1)
                nc.scalar.activation(tmp[:], tmp[:], ACT.Exp).then_inc(z_exp, 1)

            def log_sigmoid_ln(b):
                act.wait_ge(z_exp, b + 1)
                nc.scalar.activation(tmp[:], tmp[:], ACT.Ln, bias=1.0).then_inc(z_log, 1)

            def decay_out(b, i):
                act.wait_ge(cum_done, 2 * b + i + 1)
                nc.scalar.activation(tmp[:, i], ps[SMALL][:], ACT.Exp).then_inc(decay, 1)

            def gamma_out(b):
                act.wait_ge(gm_done, b + 1)
                if not is_first(b):
                    act.wait_ge(s_updated, 2 * NCH * b)
                nc.scalar.activation(gamma[:].rearrange("p f c -> p (f c)"), ps[SMALL][:, 0:2 * NCH],
                                     ACT.Exp).then_inc(gamma_ready, 1)

            def gla(b):
                tail = not is_first(b)
                nxt = not is_last(b)
                if tail:
                    head_squares(b - 1, 0)
                ka_out(b, 0)
                ka_out(b, 1)
                if tail:
                    head_squares(b - 1, 1)
                    head_rms(b - 1, 0)
                ka_out(b, 2)
                ka_out(b, 3)
                if tail:
                    head_rms(b - 1, 1)
                a_out(b)
                if tail:
                    head_squares(b - 1, 2)
                v_out(b, 0)
                v_out(b, 1)
                if tail:
                    head_squares(b - 1, 3)
                    head_rms(b - 1, 2)
                v_out(b, 2)
                log_sigmoid(b)
                log_sigmoid_ln(b)
                if tail:
                    head_rms(b - 1, 3)
                if nxt:
                    x_squares(b + 1, range(4))
                v_out(b, 3)
                if nxt:
                    x_squares(b + 1, (4, 5))
                q_out(b, 0)
                decay_out(b, 0)
                if nxt:
                    x_squares(b + 1, (6, 7))
                q_out(b, 1)
                decay_out(b, 1)
                gamma_out(b)
                if nxt:
                    x_sum_out(b + 1)
                    g_out(b, 0)
                    x_rms(b + 1)
                else:
                    g_out(b, 0)
                g_out(b, 1)
                g_out(b, 2)
                split_hi(b + 1, raw, GLA)
                g_out(b, 3)

            def conv(b):
                for j in range(4):
                    if is_first(b) and j == 0:
                        head_squares(NB - 1, 0)
                    if is_first(b) and j == 1:
                        head_rms(NB - 1, 3)
                    wait_tile(act, CONV, b, 4 * j)
                    if not (is_first(b) and j == 0):
                        act.wait_ge(conv_step, 7 * (4 * b + j - 1) + C_U)
                    nc.scalar.activation(ccs[:], ps[TURN[(4 * j) % 8]][:], ACT.Copy).then_inc(cc_copied, 1)
                    if is_first(b) and j == 0:
                        head_squares(NB - 1, 1)
                        head_rms(NB - 1, 0)
                        head_rms(NB - 1, 1)
                        head_squares(NB - 1, 2)
                    wait_tile(act, CONV, b, 4 * j + 2)
                    if not (is_first(b) and j == 0):
                        act.wait_ge(conv_step, 7 * (4 * b + j - 1) + C_DONE)
                    nc.scalar.activation(sgc[:], ps[TURN[(4 * j + 2) % 8]][:], ACT.Silu).then_inc(silu_ready, 1)
                    if is_first(b) and j == 0:
                        head_rms(NB - 1, 2)
                        head_squares(NB - 1, 3)
                split_hi(NB + b + 1, raw, OUT if is_last(b) else CONV)

            def out_proj(b):
                if is_last(b):
                    split_p_hi(0)
                split_hi(2 * NB + b + 1, raw, OUT)

            def split_p_hi(b):
                act.wait_ge(p_loaded, 16 * (b + 1))
                if not is_first(b):
                    wait_tile(act, GATE, b - 1, TILES[GATE] - 2)
                for k in range(PLE_K):
                    nc.scalar.activation(PH[:, k], p_raw[:, k], ACT.Copy).then_inc(p_hi, 1)

            def gate(b, odd=0):
                for m in range(KT):
                    if m == KT - 1 and not is_last(b):
                        split_p_hi(b + 1)
                        split_hi(3 * NB + b + 1, raws[1 - odd], GATE)
                    wait_tile(act, GATE, b, 2 * m + 1)
                    if not (is_first(b) and m < 2):
                        act.wait_ge(gated, 8 * b + m - 1)
                    nc.scalar.activation(gt[:, m % 2], ps[m % 3][:], ACT.Sigmoid,
                                         bias=vec[:, V_BG + m:V_BG + m + 1]).then_inc(gate_ready, 1)
                    if m == 0 and not is_first(b):
                        out_rms(b - 1)
                    act.wait_ge(mixed, 8 * b + m + 1)
                    if not (is_first(b) and m < 2):
                        act.wait_ge(out_sum, 8 * b + m - 1)
                    nc.scalar.activation(osq[:, m % 2], raws[odd][:, m], ACT.Square).then_inc(out_sq, 1)

            def out_rms(b):
                act.wait_ge(out_mean, b + 1)
                nc.scalar.activation(R[:], ps[STAT][:], ACT.Sqrt, bias=eps[:], scale=1.0 / D_MODEL).then_inc(
                    out_root, 1)

            act.wait_ge(memsets, 5)
            nc.scalar.activation(warm[:], eps[:], ACT.Sqrt)
            x_squares(0, range(KT))
            x_rms(0)
            act.wait_ge(consts_loaded, 80)
            nc.scalar.activation(suffix[:], mask[:, 0:P], ACT.Copy).then_inc(suffix_ready, 1)
            for k in range(KT):
                act.wait_ge(first_n, k + 1)
                nc.scalar.activation(XH[:, k, HALF_A], raw[:, k, HALF_A], ACT.Copy).then_inc(first_hi, 1)
            for i in range(1, 4):
                act.wait_ge(early_loaded[2 + i], 16)
                nc.scalar.activation(WH[:, i], early_v[i].rearrange("p (k c) -> p k c", k=KT), ACT.Copy).then_inc(
                    v_hi, 1)
            for k in range(KT):
                act.wait_ge(n_ready, k + 1)
                nc.scalar.activation(XH[:, k, HALF_B], raw[:, k, HALF_B], ACT.Copy).then_inc(x_hi, 1)
            over_blocks(act, gla, apart=2)
            over_blocks(act, conv)
            over_blocks(act, out_proj)
            for c in range(2):
                act.wait_ge(y_stored[c], 16 * 4 * NB)
            over_blocks(act, gate, pair=True)
            out_rms(NB - 1)

        @block.vector
        def _(dve):
            def split_lo(step, src):
                for k in range(KT):
                    dve.wait_ge(x_hi, 8 * step + k + 1)
                    nc.vector.tensor_tensor(XL[:, k], src[:, k], XH[:, k].bitcast(F32), ALU.subtract).then_inc(
                        x_lo, 1)

            def x_sums(s, ks):
                for k in ks:
                    dve.wait_ge(x_sq, 8 * s + k + 1)
                    if k > 1:
                        dve.wait_ge(x_sum, 7 * s + k - 1)
                    elif s > 0:
                        dve.wait_ge(r_stored, 16 * s)
                    nc.vector.tensor_tensor(R[:], sq[:, 0] if k == 1 else R[:], sq[:, k % 2], ALU.add).then_inc(
                        x_sum, 1)

            def x_split_1():
                dve.wait_ge(x_sum_hi, 1)
                nc.vector.tensor_tensor(R_lo[:], R[:], sum_hi[:].bitcast(F32), ALU.subtract).then_inc(x_split, 1)

            def x_recip(s):
                dve.wait_ge(x_root, s + 1)
                nc.vector.reciprocal(R[:], R[:]).then_inc(x_rstd, 1)

            def normalise(step, ks):
                for k in ks:
                    if k % 2 == 0:
                        dve.wait_ge(raw_loaded[k // 2], 16 * (step + 1))
                    nc.vector.scalar_tensor_tensor(out=raw[:, k], in0=raw[:, k],
                                                   scalar=vec[:, V_NORM + k:V_NORM + k + 1], in1=R[:],
                                                   op0=ALU.mult, op1=ALU.mult).then_inc(n_ready, 1)

            def split_squares(b, h):
                dve.wait_ge(head_sq, 4 * b + h + 1)
                nc.vector.tensor_tensor(hsq_lo[:], hsq[:], sum_hi[:].bitcast(F32), ALU.subtract).then_inc(
                    head_split, 1)

            def head(b, h):
                n = 4 * b + h
                pair, half = h // 2, h % 2
                tokens = slice(half * TB // 2, (half + 1) * TB // 2)
                flat = y_sb[:, h % 2].rearrange("p (h t) -> p h t", h=2)
                dve.wait_ge(head_root, n + 1)
                nc.vector.reciprocal(rt[:], rt[:]).then_inc(head_step, 1)
                dve.wait_ge(head_step, 3 * n + H_RECIP)
                if not (is_first(b) and h < 2):
                    dve.wait_ge(y_stored[h % 2], 16 * (2 * b + h // 2))
                nc.vector.scalar_tensor_tensor(out=y_sb[:, h % 2], in0=ps[O_BANK[h % 2]][:],
                                               scalar=vec[:, V_GLA:V_GLA + 1], in1=rt[:],
                                               op0=ALU.mult, op1=ALU.mult).then_inc(head_step, 1)
                dve.wait_ge(head_step, 3 * n + H_SCALED)
                dve.wait_ge(evacuated, 14 * b + 12 + 2 * pair)
                nc.vector.tensor_tensor(flat, flat, sg[:, 2 * pair:2 * pair + 2, tokens], ALU.mult).then_inc(
                    head_step, 1)

            def add_bias(b, i):
                dve.wait_ge(z_done, 2 * b + i + 1)
                if i == 0 and not is_first(b):
                    dve.wait_ge(gm_done, b)
                nc.vector.tensor_tensor(L[:, 2 * i:2 * i + 2].rearrange("p t c -> p (t c)"), ps[SMALL][:],
                                        bias2[:], ALU.add).then_inc(z_ready, 1)

            def minus_abs(b):
                dve.wait_ge(z_ready, 2 * b + 2)
                if not is_first(b):
                    dve.wait_ge(kdec, 2 * b)
                z = L[:].rearrange("p t c -> p (t c)")
                nc.vector.scalar_tensor_tensor(out=tmp[:].rearrange("p i c -> p (i c)"), in0=z, scalar=-1.0,
                                               in1=z, op0=ALU.mult, op1=ALU.min).then_inc(z_neg, 1)

            def log_decay(b):
                dve.wait_ge(z_log, b + 1)
                z = L[:].rearrange("p t c -> p (t c)")
                nc.vector.scalar_tensor_tensor(out=z, in0=z, scalar=0.0,
                                               in1=tmp[:].rearrange("p i c -> p (i c)"),
                                               op0=ALU.min, op1=ALU.subtract).then_inc(loga, 1)

            def split_decay(b, i):
                if not is_first(b):
                    dve.wait_ge(y_stored[i], 16 * 2 * b)
                z = L[:, 2 * i:2 * i + 2].rearrange("p t c -> p (t c)")
                dve.wait_ge(loga, b + 1)
                nc.vector.tensor_copy(L_hi[:, i], z).then_inc(loga_hi, 1)
                dve.wait_ge(loga_hi, 2 * b + i + 1)
                nc.vector.tensor_tensor(L_lo[:, i], z, L_hi[:, i].bitcast(F32), ALU.subtract).then_inc(
                    loga_split, 1)

            def decay_k(b, i):
                dve.wait_ge(decay, 2 * b + i + 1)
                k = ka_sb[:, 2 * i:2 * i + 2, 0:QK]
                nc.vector.tensor_tensor(k, k, tmp[:, i].rearrange("p (t c) -> p t c", t=2), ALU.mult).then_inc(
                    kdec, 1)

            def state(b, ch):
                dve.wait_ge(ds_done, NCH * b + ch + 1)
                if ch == 0:
                    dve.wait_ge(gamma_ready, b + 1)
                    if not is_first(b):
                        dve.wait_ge(o_done, HEADS * b)
                if not (is_first(b) and ch == 0):
                    dve.wait_ge(s_updated, 2 * (NCH * b + ch))
                for f in range(2):
                    nc.vector.scalar_tensor_tensor(out=hist[:, ch, f], in0=hist[:, (ch - 1) % NCH, f],
                                                   scalar=gamma[:, f, ch:ch + 1],
                                                   in1=ps[DS_BANK[ch % 2]][:, f * DV:f * DV + DV],
                                                   op0=ALU.mult, op1=ALU.add).then_inc(s_updated, 1)

            def gla(b):
                tail = not is_first(b)
                nxt = not is_last(b)
                if tail:
                    split_squares(b - 1, 0)
                    split_squares(b - 1, 1)
                    head(b - 1, 0)
                    head(b - 1, 1)
                add_bias(b, 0)
                if tail:
                    split_squares(b - 1, 2)
                add_bias(b, 1)
                minus_abs(b)
                if tail:
                    split_squares(b - 1, 3)
                    head(b - 1, 2)
                if is_first(b):
                    x_sums(1, range(1, 4))
                log_decay(b)
                if tail:
                    head(b - 1, 3)
                split_decay(b, 0)
                split_decay(b, 1)
                if is_first(b):
                    x_sums(1, range(4, 6))
                decay_k(b, 0)
                if is_first(b):
                    x_sums(1, range(6, 8))
                    x_split_1()
                decay_k(b, 1)
                if nxt:
                    x_recip(b + 1)
                    dve.wait_ge(x_rstd, b + 2)
                else:
                    dve.wait_ge(r_loaded, 16)
                normalise(b + 1, range(0, 2))
                state(b, 0)
                state(b, 1)
                normalise(b + 1, range(2, 6))
                state(b, 2)
                state(b, 3)
                normalise(b + 1, range(6, 8))
                for ch in range(4, NCH):
                    state(b, ch)
                split_lo(b + 1, raw)

            def conv(b):
                for j in range(4):
                    n = 4 * b + j
                    if not is_first(b):
                        dve.wait_ge(conv_step, 7 * (n - 4) + C_W2)
                        nc.vector.tensor_copy(u[:, j, 0:2], u[:, j, TB:TB + 2]).then_inc(conv_step, 1)
                    else:
                        nc.vector.memset(u[:, j, 0:2], 0.0).then_inc(conv_step, 1)
                    if is_first(b) and j == 0:
                        split_squares(NB - 1, 0)
                        split_squares(NB - 1, 1)
                        head(NB - 1, 0)
                        head(NB - 1, 1)
                        split_squares(NB - 1, 2)
                    dve.wait_ge(conv_step, 7 * n + C_CARRY)
                    wait_tile(dve, CONV, b, 4 * j + 1)
                    dve.wait_ge(cc_copied, n + 1)
                    nc.vector.tensor_tensor(u[:, j, 2:2 + TB], ccs[:], ps[TURN[(4 * j + 1) % 8]][:],
                                            ALU.mult).then_inc(conv_step, 1)
                    dve.wait_ge(conv_step, 7 * n + C_U)
                    w = V_CW + 3 * j
                    nc.vector.tensor_scalar(cv[:], u[:, j, 0:TB], vec[:, w:w + 1],
                                            vec[:, V_CB + j:V_CB + j + 1], ALU.mult, ALU.add).then_inc(conv_step, 1)
                    for i in (1, 2):
                        dve.wait_ge(conv_step, 7 * n + C_W0 + i - 1)
                        nc.vector.scalar_tensor_tensor(out=cv[:], in0=u[:, j, i:i + TB],
                                                       scalar=vec[:, w + i:w + i + 1], in1=cv[:],
                                                       op0=ALU.mult, op1=ALU.add).then_inc(conv_step, 1)
                    if is_first(b) and j == 0:
                        head(NB - 1, 2)
                        split_squares(NB - 1, 3)
                    if j == 3:
                        split_lo(NB + b + 1, raw)
                    wait_tile(dve, CONV, b, 4 * j + 3)
                    dve.wait_ge(conv_step, 7 * n + C_W2)
                    nc.vector.tensor_tensor(cv[:], cv[:], ps[TURN[(4 * j + 3) % 8]][:], ALU.mult).then_inc(
                        conv_step, 1)
                    if is_first(b) and j == 0:
                        head(NB - 1, 3)
                    dve.wait_ge(conv_step, 7 * n + C_GATED)
                    dve.wait_ge(silu_ready, n + 1)
                    dve.wait_ge(y_stored[j % 2], 16 * (2 * NB + 2 * b + j // 2))
                    nc.vector.tensor_tensor(y_sb[:, j % 2], cv[:], sgc[:], ALU.mult).then_inc(conv_step, 1)
                    if j == 1 and not is_last(b):
                        dve.wait_ge(r_loaded, 16 * (b + 2))
                        normalise(NB + b + 1, range(KT))

            def out_proj(b):
                for m in range(KT):
                    if m == KT - 1:
                        if is_last(b):
                            split_p_lo(0)
                        split_lo(2 * NB + b + 1, raw)
                    wait_tile(dve, OUT, b, m)
                    dve.wait_ge(xt_loaded[m % 4], 16 * (2 * b + m // 4 + 1))
                    nc.vector.tensor_tensor(xt[:, m % 4], xt[:, m % 4], ps[TURN[m]][:], ALU.add).then_inc(
                        h_ready, 1)

            def split_p_lo(b):
                dve.wait_ge(p_hi, 2 * (b + 1))
                for k in range(PLE_K):
                    nc.vector.tensor_tensor(PL[:, k], p_raw[:, k], PH[:, k].bitcast(F32), ALU.subtract).then_inc(
                        p_lo, 1)

            def gate(b, odd=0):
                def add_square(m):
                    dve.wait_ge(out_sq, 8 * b + m + 1)
                    if m == 0:
                        if is_first(b):
                            for c in range(4):
                                dve.wait_ge(h_stored[c], 16 * 2 * NB)
                        else:
                            dve.wait_ge(out_mean, b)
                        nc.vector.tensor_copy(acc[:], osq[:, 0]).then_inc(out_sum, 1)
                    else:
                        dve.wait_ge(out_sum, 8 * b + m)
                        nc.vector.tensor_tensor(acc[:], acc[:], osq[:, m % 2], ALU.add).then_inc(out_sum, 1)

                for m in range(KT):
                    if m == KT - 1 and not is_last(b):
                        split_p_lo(b + 1)
                        split_lo(3 * NB + b + 1, raws[1 - odd])
                    wait_tile(dve, GATE, b, 2 * m)
                    dve.wait_ge(gate_ready, 8 * b + m + 1)
                    if not (is_first(b) and m == 0):
                        dve.wait_ge(mixed, 8 * b + m)
                    nc.vector.tensor_tensor(t_sb[:], gt[:, m % 2], ps[3 + m % 3][:], ALU.mult).then_inc(gated, 1)
                    dve.wait_ge(gated, 8 * b + m + 1)
                    nc.vector.tensor_tensor(raws[odd][:, m], raws[odd][:, m], t_sb[:], ALU.add).then_inc(mixed, 1)
                    if m >= 1:
                        add_square(m - 1)
                    if m == 0 and not is_first(b):
                        final_norm(b - 1, 1 - odd)
                if not is_last(b):
                    add_square(KT - 1)
                    dve.wait_ge(out_sum, 8 * (b + 1))
                    nc.vector.tensor_copy(acc_hi[:], acc[:]).then_inc(out_sum_hi, 1)
                    dve.wait_ge(out_sum_hi, b + 1)
                    nc.vector.tensor_tensor(acc_lo[:], acc[:], acc_hi[:].bitcast(F32), ALU.subtract).then_inc(
                        out_split, 1)

            def final_norm(b, odd):
                dve.wait_ge(out_root, b + 1)
                nc.vector.reciprocal(R[:], R[:]).then_inc(out_rstd, 1)
                dve.wait_ge(out_rstd, b + 1)
                for m in range(KT):
                    nc.vector.scalar_tensor_tensor(out=raws[odd][:, m], in0=raws[odd][:, m],
                                                   scalar=vec[:, V_FIN + m:V_FIN + m + 1], in1=R[:],
                                                   op0=ALU.mult, op1=ALU.mult).then_inc(out_norm, 1)

            dve.wait_ge(memsets, 5)
            x_sums(0, range(1, KT))
            dve.wait_ge(consts_loaded, 80)
            dve.wait_ge(x_root, 1)
            for half, rstd, n_done, hi_done, lo_done in ((HALF_A, first_rstd, first_n, first_hi, first_lo),
                                                         (HALF_B, x_rstd, n_ready, x_hi, x_lo)):
                nc.vector.reciprocal(R[:, half], R[:, half]).then_inc(rstd, 1)
                dve.wait_ge(rstd, 1)
                for k in range(KT):
                    if k % 2 == 0:
                        dve.wait_ge(raw_loaded[k // 2], 16)
                    nc.vector.scalar_tensor_tensor(out=raw[:, k, half], in0=raw[:, k, half],
                                                   scalar=vec[:, V_NORM + k:V_NORM + k + 1], in1=R[:, half],
                                                   op0=ALU.mult, op1=ALU.mult).then_inc(n_done, 1)
                dve.wait_ge(lo_done, FIRST_LO)
                for k in range(FIRST_LO, KT):
                    dve.wait_ge(hi_done, k + 1)
                    nc.vector.tensor_tensor(XL[:, k, half], raw[:, k, half], XH[:, k, half].bitcast(F32),
                                            ALU.subtract).then_inc(lo_done, 1)
            for i in range(4 - V_BY_DVE, 4):
                dve.wait_ge(v_hi, i)
                nc.vector.tensor_tensor(WL[:, i], early_v[i].rearrange("p (k c) -> p k c", k=KT),
                                        WH[:, i].bitcast(F32), ALU.subtract).then_inc(v_lo, 1)
            over_blocks(dve, gla, apart=2)
            over_blocks(dve, conv)
            over_blocks(dve, out_proj)
            over_blocks(dve, gate, pair=True)
            final_norm(NB - 1, 1)


def kernel(x, p, norm_w, w_in, w_alpha_up, b_alpha, gla_norm_w, conv_w, conv_b,
           w_out, w_ple, w_ple_gate, b_ple_gate, final_norm_w):
    import numpy as np
    import concourse.bacc as bacc
    from concourse.bass_utils import run_bass_kernel_spmd

    def blocks(a):
        return np.ascontiguousarray(np.asarray(a).reshape(NB, TB, -1, P).transpose(0, 3, 2, 1))

    def tiles(w):
        w = np.asarray(w)
        return np.ascontiguousarray(w.reshape(w.shape[0] // P, P, -1, P).transpose(2, 1, 0, 3)).reshape(
            w.shape[1] // P, P, -1)

    def cols(v):
        return np.asarray(v).reshape(-1, P).T

    w = np.asarray(w_in)[0]
    q, k, v, g, a, cb, cc, cu, gc = np.split(w, np.cumsum([256, 256, 512, 512, 16, 512, 512, 512]), axis=1)
    ka = np.concatenate([k, a], axis=1).reshape(KT, P, KA).transpose(1, 0, 2)
    conv = np.stack([m.reshape(D_MODEL, 4, P) for m in (cc, cu, gc, cb)], axis=2).reshape(D_MODEL, 4 * 512)
    ple = np.asarray(w_ple)[0].reshape(PLE_K, P, D_MODEL)

    r = np.arange(P)
    same = (r[:, None] // CHUNK) == (r[None, :] // CHUNK)
    tau = 16.0
    masks = np.concatenate([(same & (r[:, None] > r[None, :])) / tau,
                            ((r[:, None] // CHUNK) == np.arange(2)[None, :]) / tau, np.eye(P)],
                           axis=1).astype(np.float32)
    cw = np.asarray(conv_w)[0].reshape(3, 4, P).transpose(2, 1, 0).reshape(P, 12)
    vectors = np.concatenate([cols(np.asarray(norm_w)[0]), cols(np.asarray(gla_norm_w)[0]), cw,
                              cols(np.asarray(conv_b)[0]), cols(np.asarray(b_ple_gate)[0]),
                              cols(final_norm_w)], axis=1)
    ba = np.asarray(b_alpha)[0]
    arrays = {
        "xb": blocks(np.asarray(x)[0]), "pb": blocks(np.asarray(p)[0, 0]), "w_ka": ka,
        "w_in": tiles(np.concatenate([v, q, g, conv], axis=1)), "w_out": tiles(np.asarray(w_out)[0]),
        "w_gate": tiles(np.asarray(w_ple_gate)[0]), "w_ple": ple, "w_up": np.asarray(w_alpha_up)[0],
        "b_alpha": np.broadcast_to(np.concatenate([ba, ba]), (P, 2 * QK)), "vectors": vectors, "masks": masks,
    }
    arrays = {f"{n}_dram": np.ascontiguousarray(a) for n, a in arrays.items()}

    nc = bacc.Bacc("TRN2", target_bir_lowering=False, num_devices=1, dynamic_dma_scratch_size=2048)
    args = [nc.dram_tensor(n, a.shape, F32, kind="ExternalInput").ap() for n, a in arrays.items()]
    args.append(nc.dram_tensor("out_dram", (NB, P, KT, TB), F32, kind="ExternalOutput").ap())
    args.append(nc.dram_tensor("y_scratch", (NB, P, KT, TB), F32).ap())
    args.append(nc.dram_tensor("h_scratch", (NB, P, KT, TB), F32).ap())
    args.append(nc.dram_tensor("r_scratch", (NB, P, TB), F32).ap())
    build(nc, *args)
    res = run_bass_kernel_spmd(nc, [arrays], core_ids=[0])
    o = res.results[0]["out_dram"]
    return o.transpose(0, 3, 2, 1).reshape(1, SEQ, D_MODEL)
```
